# Optimizing a Trainium2 kernel written in Bass

```python
import numpy as np
import jax, jax.numpy as jnp
from jax import lax

D_MODEL = 1024
BATCH = 1
SEQ = 512
DEPTH = 1

D_CONV = D_MODEL
CONV_K = 3
HEAD_DIM = 64
N_HEADS = D_MODEL // HEAD_DIM
N_KV_HEADS = 4
GROUP = N_HEADS // N_KV_HEADS
D_ATTN = N_HEADS * HEAD_DIM
D_KV = N_KV_HEADS * HEAD_DIM
WINDOW = 128
BLOCK = 128
ROPE_THETA = 10000.0
D_FF = 2816
N_MOD = 9
EPS = 1e-6
ADA_INIT = 0.5
NEG_INF = -1e30

IN_SPLITS = [D_CONV, D_CONV, D_CONV, D_ATTN, D_KV, D_KV, D_MODEL, D_MODEL]
IN_OFFSETS = [int(o) for o in np.cumsum(IN_SPLITS)[:-1]]
D_IN = int(sum(IN_SPLITS))


def rms_norm(x, g):
    xf = x.astype(jnp.float32)
    y = xf * lax.rsqrt(jnp.mean(xf * xf, axis=-1, keepdims=True) + EPS)
    return (y * g.astype(jnp.float32)).astype(x.dtype)

def modulate(h, shift, scale):
    return h * (1 + scale[:, None, :]) + shift[:, None, :]

def swiglu(h, w_gu, w_down):
    a, b = jnp.split(h @ w_gu, 2, axis=-1)
    return (jax.nn.silu(a) * b) @ w_down

def rope_tables(seq):
    inv = 1.0 / (ROPE_THETA ** (jnp.arange(0, HEAD_DIM, 2, dtype=jnp.float32) / HEAD_DIM))
    ang = jnp.arange(seq, dtype=jnp.float32)[:, None] * inv[None, :]
    return jnp.cos(ang), jnp.sin(ang)

def apply_rope(t, cos, sin):
    t1, t2 = jnp.split(t.astype(jnp.float32), 2, axis=-1)
    c = cos[None, :, None, :]
    s = sin[None, :, None, :]
    return jnp.concatenate([t1 * c - t2 * s, t2 * c + t1 * s], axis=-1).astype(t.dtype)

def short_conv(u, w):
    s = u.shape[1]
    up = jnp.pad(u, ((0, 0), (CONV_K - 1, 0), (0, 0)))
    out = up[:, 0:s] * w[0]
    for j in range(1, CONV_K):
        out = out + up[:, j:j + s] * w[j]
    return out

def sliding_window_attention(q, k, v, sinks):
    bsz, s, _, _ = q.shape
    nb = s // BLOCK
    qb = q.reshape(bsz, nb, BLOCK, N_KV_HEADS, GROUP, HEAD_DIM)

    def band(t):
        tp = jnp.pad(t, ((0, 0), (BLOCK, 0), (0, 0), (0, 0)))
        tp = tp.reshape(bsz, nb + 1, BLOCK, N_KV_HEADS, HEAD_DIM)
        return jnp.concatenate([tp[:, :-1], tp[:, 1:]], axis=2)

    kb, vb = band(k), band(v)
    scores = jnp.einsum('bnqhgd,bnkhd->bnhgqk', qb, kb,
                        preferred_element_type=jnp.float32) * (HEAD_DIM ** -0.5)
    qi = jnp.arange(BLOCK)[:, None]
    kj = jnp.arange(2 * BLOCK)[None, :]
    diff = BLOCK + qi - kj
    in_window = (diff >= 0) & (diff < WINDOW)
    k_pos = (jnp.arange(nb)[:, None] - 1) * BLOCK + jnp.arange(2 * BLOCK)[None, :]
    valid = in_window[None] & (k_pos >= 0)[:, None, :]
    scores = jnp.where(valid[None, :, None, None], scores, NEG_INF)
    sink = sinks.astype(jnp.float32).reshape(N_KV_HEADS, GROUP)[None, None, :, :, None, None]
    m = jnp.maximum(jnp.max(scores, axis=-1, keepdims=True), sink)
    p = jnp.exp(scores - m)
    denom = jnp.sum(p, axis=-1, keepdims=True) + jnp.exp(sink - m)
    probs = (p / denom).astype(v.dtype)
    out = jnp.einsum('bnhgqk,bnkhd->bnqhgd', probs, vb)
    return out.reshape(bsz, s, D_ATTN)

def first_inputs(seed: int = 0) -> dict:
    key = jax.random.key(seed)
    ks = jax.random.split(key, 24)
    f32 = jnp.float32

    def nrm(k, shape, fan_in, mult=1.0):
        return jax.random.normal(k, shape, f32) * (mult * fan_in ** -0.5)

    def gain(k, shape):
        return 1.0 + 0.05 * jax.random.normal(k, shape, f32)

    L = DEPTH
    return {
        "x": jax.random.normal(ks[0], (BATCH, SEQ, D_MODEL), f32),
        "c": jax.random.normal(ks[1], (BATCH, D_MODEL), f32),
        "w_ada": nrm(ks[2], (L, D_MODEL, N_MOD * D_MODEL), D_MODEL, ADA_INIT),
        "b_ada": 0.02 * jax.random.normal(ks[3], (L, N_MOD * D_MODEL), f32),
        "g_ffn1": gain(ks[4], (L, D_MODEL)),
        "w1_gu": nrm(ks[5], (L, D_MODEL, 2 * D_FF), D_MODEL),
        "w1_down": nrm(ks[6], (L, D_FF, D_MODEL), D_FF),
        "g_mix": gain(ks[7], (L, D_MODEL)),
        "w_in": nrm(ks[8], (L, D_MODEL, D_IN), D_MODEL),
        "conv_w": nrm(ks[9], (L, CONV_K, D_CONV), CONV_K),
        "w_conv_proj": nrm(ks[10], (L, D_CONV, D_MODEL), D_CONV),
        "w_attn_proj": nrm(ks[11], (L, D_ATTN, D_MODEL), D_ATTN),
        "sinks": jax.random.normal(ks[12], (L, N_HEADS), f32),
        "w_out": nrm(ks[13], (L, D_MODEL, D_MODEL), D_MODEL),
        "g_ffn2": gain(ks[14], (L, D_MODEL)),
        "w2_gu": nrm(ks[15], (L, D_MODEL, 2 * D_FF), D_MODEL),
        "w2_down": nrm(ks[16], (L, D_FF, D_MODEL), D_FF),
        "g_final": gain(ks[17], (D_MODEL,)),
    }

def first_block(x, c, w_ada, b_ada, g_ffn1, w1_gu, w1_down, g_mix, w_in, conv_w,
              w_conv_proj, w_attn_proj, sinks, w_out, g_ffn2, w2_gu, w2_down, g_final):
    bsz, s, _ = x.shape
    cos, sin = rope_tables(s)
    c_act = jax.nn.silu(c)
    for l in range(DEPTH):
        mods = jnp.split(c_act @ w_ada[l] + b_ada[l], N_MOD, axis=-1)
        sh1, sc1, gt1, sh2, sc2, gt2, sh3, sc3, gt3 = mods

        h = modulate(rms_norm(x, g_ffn1[l]), sh1, sc1)
        x = x + 0.5 * gt1[:, None, :] * swiglu(h, w1_gu[l], w1_down[l])

        h = modulate(rms_norm(x, g_mix[l]), sh2, sc2)
        proj = h @ w_in[l]
        b_g, c_g, u, q, k, v, z_conv, z_attn = jnp.split(proj, IN_OFFSETS, axis=-1)

        y_conv = (b_g * short_conv(c_g * u, conv_w[l])) @ w_conv_proj[l]

        q = apply_rope(q.reshape(bsz, s, N_HEADS, HEAD_DIM), cos, sin)
        k = apply_rope(k.reshape(bsz, s, N_KV_HEADS, HEAD_DIM), cos, sin)
        v = v.reshape(bsz, s, N_KV_HEADS, HEAD_DIM)
        y_attn = sliding_window_attention(q, k, v, sinks[l]) @ w_attn_proj[l]

        merged = jax.nn.sigmoid(z_conv) * y_conv + jax.nn.sigmoid(z_attn) * y_attn
        x = x + gt2[:, None, :] * (merged @ w_out[l])

        h = modulate(rms_norm(x, g_ffn2[l]), sh3, sc3)
        x = x + 0.5 * gt3[:, None, :] * swiglu(h, w2_gu[l], w2_down[l])

    return rms_norm(x, g_final)


MEM_LEN = 256
MIX_WIDTH = D_MODEL
HGRN_WIDTH = MIX_WIDTH // 2
MLSTM_WIDTH = MIX_WIDTH - HGRN_WIDTH
HGRN_HEADS = 4
HGRN_HEAD_DIM = HGRN_WIDTH // HGRN_HEADS
MLSTM_HEADS = 4
MLSTM_HEAD_DIM = MLSTM_WIDTH // MLSTM_HEADS
CONV_WIDTH = 5
XATTN_HEADS = 4
XATTN_HEAD_DIM = D_MODEL // XATTN_HEADS
D_FF_2 = 4 * D_MODEL
CHUNK = 64
NORM_EPS = 1e-6
MLSTM_FGATE_BIAS = 3.0
IN_SPLITS_2 = (HGRN_WIDTH, HGRN_WIDTH, HGRN_WIDTH, HGRN_WIDTH, HGRN_WIDTH,
             MLSTM_WIDTH, MLSTM_WIDTH, MLSTM_WIDTH, MLSTM_WIDTH,
             MLSTM_HEADS, MLSTM_HEADS, MLSTM_HEADS, MLSTM_HEADS)
D_IN_2 = 5 * HGRN_WIDTH + 4 * MLSTM_WIDTH + 4 * MLSTM_HEADS


def rmsnorm(x, g):
    x32 = x.astype(jnp.float32)
    y = x32 * lax.rsqrt(jnp.mean(x32 * x32, axis=-1, keepdims=True) + NORM_EPS)
    return (y * g.astype(jnp.float32)).astype(x.dtype)

def head_rmsnorm(h, g, n_heads):
    b, s, w = h.shape
    h32 = h.astype(jnp.float32).reshape(b, s, n_heads, w // n_heads)
    h32 = h32 * lax.rsqrt(jnp.mean(h32 * h32, axis=-1, keepdims=True) + NORM_EPS)
    return (h32.reshape(b, s, w) * g.astype(jnp.float32)).astype(h.dtype)

def split_cols(t, sizes):
    idx = np.cumsum(np.array(sizes))[:-1].tolist()
    return jnp.split(t, idx, axis=-1)

def to_heads(t, n_heads):
    b, s, w = t.shape
    return t.reshape(b, s, n_heads, w // n_heads).transpose(0, 2, 1, 3)

def from_heads(t):
    b, h, s, d = t.shape
    return t.transpose(0, 2, 1, 3).reshape(b, s, h * d)

def to_chunks(t):
    b, h, s = t.shape[:3]
    t = t.reshape(b, h, s // CHUNK, CHUNK, *t.shape[3:])
    return jnp.moveaxis(t, 2, 0)

def from_chunks(t):
    t = jnp.moveaxis(t, 0, 2)
    b, h, n, c = t.shape[:4]
    return t.reshape(b, h, n * c, *t.shape[4:])

def flip_seq(t):
    return jnp.flip(t, axis=2)

def hgrn2_scan(q, k, v, log_f):
    b, h, _, dk = q.shape
    dv = v.shape[-1]
    tril = jnp.tril(jnp.ones((CHUNK, CHUNK), dtype=bool))

    def step(state, xs):
        qc, kc, vc, lfc = xs
        cum = jnp.cumsum(lfc, axis=-2)
        o_inter = jnp.einsum('bhtd,bhde->bhte', qc * jnp.exp(cum), state)
        diff = cum[:, :, :, None, :] - cum[:, :, None, :, :]
        decay = jnp.exp(jnp.where(tril[:, :, None], diff, -jnp.inf))
        scores = jnp.einsum('bhtd,bhsd,bhtsd->bhts', qc, kc, decay)
        o_intra = jnp.einsum('bhts,bhse->bhte', scores, vc)
        cum_last = cum[:, :, -1:, :]
        k_dec = kc * jnp.exp(cum_last - cum)
        state = (jnp.exp(cum_last[:, :, 0, :])[..., None] * state
                 + jnp.einsum('bhsd,bhse->bhde', k_dec, vc))
        return state, o_inter + o_intra

    s0 = jnp.zeros((b, h, dk, dv), jnp.float32)
    xs = tuple(to_chunks(t.astype(jnp.float32)) for t in (q, k, v, log_f))
    _, o = lax.scan(step, s0, xs)
    return from_chunks(o)

def mlstm_scan(q, k, v, ig, log_fg):
    b, h, _, d = q.shape
    tril = jnp.tril(jnp.ones((CHUNK, CHUNK), dtype=bool))

    def step(carry, xs):
        c_st, n_st, m = carry
        qc, kc, vc, igc, lfc = xs
        cum = jnp.cumsum(lfc, axis=-1)
        log_d = cum[..., :, None] - cum[..., None, :] + igc[..., None, :]
        log_d = jnp.where(tril, log_d, -jnp.inf)
        log_inter = cum + m[..., None]
        m_t = jnp.maximum(jnp.max(log_d, axis=-1), log_inter)
        d_mat = jnp.exp(log_d - m_t[..., None])
        w_inter = jnp.exp(log_inter - m_t)
        scores = jnp.einsum('bhtd,bhsd->bhts', qc, kc) * d_mat
        num = (jnp.einsum('bhts,bhse->bhte', scores, vc)
               + w_inter[..., None] * jnp.einsum('bhtd,bhde->bhte', qc, c_st))
        den = jnp.sum(scores, axis=-1) + w_inter * jnp.einsum('bhtd,bhd->bht', qc, n_st)
        h_out = num / jnp.maximum(jnp.abs(den), jnp.exp(-m_t))[..., None]
        cum_last = cum[..., -1]
        log_w = cum_last[..., None] - cum + igc
        m_new = jnp.maximum(cum_last + m, jnp.max(log_w, axis=-1))
        carry_w = jnp.exp(cum_last + m - m_new)
        k_w = kc * jnp.exp(log_w - m_new[..., None])[..., None]
        c_st = carry_w[..., None, None] * c_st + jnp.einsum('bhsd,bhse->bhde', k_w, vc)
        n_st = carry_w[..., None] * n_st + jnp.sum(k_w, axis=-2)
        return (c_st, n_st, m_new), h_out

    init = (jnp.zeros((b, h, d, d), jnp.float32),
            jnp.zeros((b, h, d), jnp.float32),
            jnp.zeros((b, h), jnp.float32))
    xs = tuple(to_chunks(t.astype(jnp.float32)) for t in (q, k, v, ig, log_fg))
    _, hs = lax.scan(step, init, xs)
    return from_chunks(hs)

def layer_lower_bounds(logits):
    p = jax.nn.softmax(logits.astype(jnp.float32), axis=1)
    c = jnp.cumsum(p, axis=1)
    return c - c[:, :1]

def lower_bounded_log_forget(z, lb):
    z = z.astype(jnp.float32)
    return jnp.logaddexp(jnp.log(lb), jnp.log1p(-lb) + jax.nn.log_sigmoid(z))

def centred_dwconv(x, w, b):
    y = lax.conv_general_dilated(
        x, w[:, None, :], window_strides=(1,),
        padding=[(CONV_WIDTH // 2, CONV_WIDTH // 2)],
        dimension_numbers=('NWC', 'WIO', 'NWC'),
        feature_group_count=x.shape[-1])
    return y + b

def token_mixer(xn, w_in, b_in, lb_fwd, lb_bwd, conv_w, conv_b, hgrn_g, mlstm_g, w_out):
    proj = xn @ w_in + b_in
    (h_q, h_f_fwd, h_f_bwd, h_i, h_g,
     m_q, m_k, m_v, m_o,
     m_ig_fwd, m_ig_bwd, m_fg_fwd, m_fg_bwd) = split_cols(proj, IN_SPLITS_2)

    q_h = to_heads(jax.nn.silu(h_q), HGRN_HEADS)
    v_h = to_heads(h_i, HGRN_HEADS)
    lf_fwd = to_heads(lower_bounded_log_forget(h_f_fwd, lb_fwd), HGRN_HEADS)
    lf_bwd = to_heads(lower_bounded_log_forget(h_f_bwd, lb_bwd), HGRN_HEADS)
    k_fwd = -jnp.expm1(lf_fwd)
    k_bwd = -jnp.expm1(lf_bwd)
    o_h = (hgrn2_scan(q_h, k_fwd, v_h, lf_fwd)
           + flip_seq(hgrn2_scan(flip_seq(q_h), flip_seq(k_bwd), flip_seq(v_h), flip_seq(lf_bwd))))
    hgrn_out = head_rmsnorm(from_heads(o_h).astype(xn.dtype), hgrn_g, HGRN_HEADS) * jax.nn.silu(h_g)

    qk = jax.nn.silu(centred_dwconv(jnp.concatenate([m_q, m_k], axis=-1), conv_w, conv_b))
    m_q, m_k = jnp.split(qk, 2, axis=-1)
    q_m = to_heads(m_q, MLSTM_HEADS)
    k_m = to_heads(m_k, MLSTM_HEADS) * (MLSTM_HEAD_DIM ** -0.5)
    v_m = to_heads(m_v, MLSTM_HEADS)
    ig_fwd = jnp.swapaxes(m_ig_fwd, 1, 2).astype(jnp.float32)
    ig_bwd = jnp.swapaxes(m_ig_bwd, 1, 2).astype(jnp.float32)
    lfg_fwd = jax.nn.log_sigmoid(jnp.swapaxes(m_fg_fwd, 1, 2).astype(jnp.float32))
    lfg_bwd = jax.nn.log_sigmoid(jnp.swapaxes(m_fg_bwd, 1, 2).astype(jnp.float32))
    h_m = (mlstm_scan(q_m, k_m, v_m, ig_fwd, lfg_fwd)
           + flip_seq(mlstm_scan(flip_seq(q_m), flip_seq(k_m), flip_seq(v_m),
                                 flip_seq(ig_bwd), flip_seq(lfg_bwd))))
    mlstm_out = head_rmsnorm(from_heads(h_m).astype(xn.dtype), mlstm_g, MLSTM_HEADS) * jax.nn.sigmoid(m_o)

    return jnp.concatenate([hgrn_out, mlstm_out], axis=-1) @ w_out

def cross_attention(xn, memn, w_q, w_kv, w_o):
    b, s, _ = xn.shape
    q = (xn @ w_q).reshape(b, s, XATTN_HEADS, XATTN_HEAD_DIM)
    k, v = jnp.split(memn @ w_kv, 2, axis=-1)
    k = k.reshape(b, -1, XATTN_HEADS, XATTN_HEAD_DIM)
    v = v.reshape(b, -1, XATTN_HEADS, XATTN_HEAD_DIM)
    scores = jnp.einsum('bqhd,bkhd->bhqk', q, k).astype(jnp.float32) * (XATTN_HEAD_DIM ** -0.5)
    p = jax.nn.softmax(scores, axis=-1).astype(v.dtype)
    o = jnp.einsum('bhqk,bkhd->bqhd', p, v).reshape(b, s, D_MODEL)
    return o @ w_o

def squared_relu_mlp(xn, w_up, w_down):
    return jnp.square(jax.nn.relu(xn @ w_up)) @ w_down

def second_inputs(seed: int = 0) -> dict:
    key = jax.random.key(seed)
    ks = jax.random.split(key, 20)

    def nrm(k, shape, scale):
        return jax.random.normal(k, shape, jnp.float32) * scale

    def gain(k, shape):
        return 1.0 + 0.05 * jax.random.normal(k, shape, jnp.float32)

    fgate_offset = jnp.concatenate([jnp.zeros((D_IN_2 - 2 * MLSTM_HEADS,), jnp.float32),
                                    jnp.full((2 * MLSTM_HEADS,), MLSTM_FGATE_BIAS, jnp.float32)])
    return {
        "x": nrm(ks[0], (BATCH, SEQ, D_MODEL), 1.0),
        "mem": nrm(ks[1], (BATCH, MEM_LEN, D_MODEL), 1.0),
        "norm_mix": gain(ks[2], (DEPTH, D_MODEL)),
        "norm_xattn": gain(ks[3], (DEPTH, D_MODEL)),
        "norm_mem": gain(ks[4], (DEPTH, D_MODEL)),
        "norm_mlp": gain(ks[5], (DEPTH, D_MODEL)),
        "norm_final": gain(ks[6], (D_MODEL,)),
        "w_in": nrm(ks[7], (DEPTH, D_MODEL, D_IN_2), D_MODEL ** -0.5),
        "b_in": nrm(ks[8], (DEPTH, D_IN_2), 0.02) + fgate_offset,
        "hgrn_lb_logits": nrm(ks[9], (2, DEPTH, HGRN_WIDTH), 0.5),
        "hgrn_norm": gain(ks[10], (DEPTH, HGRN_WIDTH)),
        "mlstm_conv_w": nrm(ks[11], (DEPTH, CONV_WIDTH, 2 * MLSTM_WIDTH), CONV_WIDTH ** -0.5),
        "mlstm_conv_b": nrm(ks[12], (DEPTH, 2 * MLSTM_WIDTH), 0.02),
        "mlstm_norm": gain(ks[13], (DEPTH, MLSTM_WIDTH)),
        "w_out": nrm(ks[14], (DEPTH, MIX_WIDTH, D_MODEL), MIX_WIDTH ** -0.5),
        "w_xq": nrm(ks[15], (DEPTH, D_MODEL, D_MODEL), D_MODEL ** -0.5),
        "w_xkv": nrm(ks[16], (DEPTH, D_MODEL, 2 * D_MODEL), D_MODEL ** -0.5),
        "w_xo": nrm(ks[17], (DEPTH, D_MODEL, D_MODEL), D_MODEL ** -0.5),
        "w_up": nrm(ks[18], (DEPTH, D_MODEL, D_FF_2), D_MODEL ** -0.5),
        "w_down": nrm(ks[19], (DEPTH, D_FF_2, D_MODEL), D_FF_2 ** -0.5),
    }

def second_block(x, mem, norm_mix, norm_xattn, norm_mem, norm_mlp, norm_final, w_in, b_in,
              hgrn_lb_logits, hgrn_norm, mlstm_conv_w, mlstm_conv_b, mlstm_norm, w_out,
              w_xq, w_xkv, w_xo, w_up, w_down):
    lb = layer_lower_bounds(hgrn_lb_logits)
    for l in range(DEPTH):
        x = x + token_mixer(rmsnorm(x, norm_mix[l]), w_in[l], b_in[l], lb[0, l], lb[1, l],
                            mlstm_conv_w[l], mlstm_conv_b[l], hgrn_norm[l], mlstm_norm[l], w_out[l])
        x = x + cross_attention(rmsnorm(x, norm_xattn[l]), rmsnorm(mem, norm_mem[l]),
                                w_xq[l], w_xkv[l], w_xo[l])
        x = x + squared_relu_mlp(rmsnorm(x, norm_mlp[l]), w_up[l], w_down[l])
    return rmsnorm(x, norm_final)


def setup_inputs(seed=0):
    out = dict(first_inputs(seed))
    for name, value in second_inputs(seed + 1).items():
        if name != "x":
            out[name + "_2"] = value
    return out


def reference(
    x, c, w_ada, b_ada, g_ffn1, w1_gu, w1_down, g_mix, w_in, conv_w, w_conv_proj, w_attn_proj,
    sinks, w_out, g_ffn2, w2_gu, w2_down, g_final, mem_2, norm_mix_2, norm_xattn_2, norm_mem_2,
    norm_mlp_2, norm_final_2, w_in_2, b_in_2, hgrn_lb_logits_2, hgrn_norm_2, mlstm_conv_w_2,
    mlstm_conv_b_2, mlstm_norm_2, w_out_2, w_xq_2, w_xkv_2, w_xo_2, w_up_2, w_down_2,
):
    x = first_block(
        x, c, w_ada, b_ada, g_ffn1, w1_gu, w1_down, g_mix, w_in, conv_w, w_conv_proj,
        w_attn_proj, sinks, w_out, g_ffn2, w2_gu, w2_down, g_final,
    )
    return second_block(
        x, mem_2, norm_mix_2, norm_xattn_2, norm_mem_2, norm_mlp_2, norm_final_2, w_in_2,
        b_in_2, hgrn_lb_logits_2, hgrn_norm_2, mlstm_conv_w_2, mlstm_conv_b_2, mlstm_norm_2,
        w_out_2, w_xq_2, w_xkv_2, w_xo_2, w_up_2, w_down_2,
    )


_drawn_inputs = setup_inputs


def setup_inputs(seed=0):
    import zlib

    import numpy as np

    out = dict(_drawn_inputs(seed))
    spreads = {}
    factors = {'g_ffn1': 5.853,
     'sinks': 8.0,
     'g_ffn2': 6.203,
     'norm_xattn_2': 8.0,
     'norm_mem_2': 7.83,
     'hgrn_norm_2': 2.776,
     'mlstm_conv_b_2': 8.0,
     'mlstm_norm_2': 3.161,
     'norm_mlp_2': 6.451}
    for name, (base, spread) in spreads.items():
        noise = np.random.default_rng([zlib.crc32(name.encode()), seed]).standard_normal(out[name].shape)
        drawn = base * np.exp(spread * noise) if base else spread * noise
        out[name] = __import__('jax').numpy.asarray(drawn.astype(out[name].dtype))
    for name, factor in factors.items():
        out[name] = (out[name] * factor).astype(out[name].dtype)
    return out
```

```python
from contextlib import ExitStack

import numpy as np
import concourse.bass as bass
from concourse import mybir

ALU = mybir.AluOpType
ACT = mybir.ActivationFunctionType
AX_X = mybir.AxisListType.X
F32 = mybir.dt.float32
F32R = mybir.dt.float32r
U8 = mybir.dt.uint8

P = 128
S = 512
D = 1024
DC = D // P
NB = S // P
EPS = 1e-6
N_MOD = 9
N_ADA = N_MOD * DC
FF = 2816
FF_PARTS = (8, 8, 6)
HD = 64
N_KV = 4
N_Q = 16
MEM = 256
NH2 = 4
LEVELS = 7
ITEMS = 2 * LEVELS + 4
EVENTS = 3 + 2 * (LEVELS + 1)
ML_STEPS = 7
MLP_PARTS = 4
SCORE_SCALE = HD ** -0.5
XATTN_SCALE = (D // NH2) ** -0.5
MLSTM_SCALE = P ** -0.5

V_FFN_LEN = 2 * (FF // P) + len(FF_PARTS) * DC
V_MIX = V_FFN_LEN
V_CONV = V_MIX + 12
V_CP = V_CONV + 24
V_AP = V_CP + 16
V_WO = V_AP + 16
V_FFN = (0, V_WO + DC)
V_GATE = V_FFN[1] + V_FFN_LEN
V_HG = V_GATE + 1
V_ML = V_HG + 5 * NH2
V_WO2 = V_ML + 4 * NH2
V_XK = V_WO2 + DC
V_XV = V_XK + DC
V_XQ = V_XV + DC
V_XO = V_XQ + DC
V_MLP = V_XO + DC
V_END = V_MLP + 2 * MLP_PARTS * DC
ADA_HEAD_N, ADA_FIRST = 2 * DC, 3 * DC
ADA_PART = (24, 40, 56, 68)


def raw_of(v):
    if v >= 60:
        return v + 72
    part = v // 24
    base, k = ADA_FIRST + 40 * part, v - 24 * part
    return base + 2 * k if k < 16 else base + 16 + k


def raw_of_ada(a):
    if a < ADA_FIRST:
        return a
    if a >= ADA_PART[3]:
        return 128 + (a - ADA_PART[3])
    part = (a - ADA_FIRST) // 16
    return ADA_FIRST + 40 * part + 2 * (a - ADA_PART[part]) + 1


def chunks_of(v):
    return FF_PARTS[2] if any(base + 60 <= v < base + V_FFN_LEN for base in V_FFN) else DC


J_FFN = (0, 46)
J_Y, J_O, J_M = 22, 30, 38
J_Y2, J_XO, J_MLP = 68, 76, 84

N_FFN1, N_MIX, N_FFN2, N_FINAL, N_MIX2, N_MEM, N_XATTN, N_MLP, N_OUT = range(9)


def columns(*names):
    at, where = 0, {}
    for name, n in names:
        where[name] = at
        at += n
    return where, at


VEC, N_VEC = columns(("c", DC), ("b_ada", N_ADA), ("gain", 9 * DC), ("conv_w", 3 * DC), ("b_in", 36), ("b_gate", 2),
                     ("lb", 8), ("hgrn_g", NH2), ("mconv_w", 5 * DC), ("mconv_b", DC), ("mlstm_g", NH2),
                     ("sinks", N_Q))
CON, N_CON = columns(("ident", P), ("ones", P), ("rot", P), ("tri", 2 * P), ("win", 2 * P), ("sel", 8 * P))
SUM, NEG_MAX, SINK, DEN, RDEN, ROW_MAX = range(6)


def build(nc, x_in, mem_in, vec_in, con_in, rope_in, mask_in, w8_in, w6_in, out):
    with ExitStack() as ctx:
        def sb(name, shape, dt=F32):
            return ctx.enter_context(nc.sbuf_tensor(name, shape, dt))

        def sem(name):
            return ctx.enter_context(nc.semaphore(name))

        bank = [ctx.enter_context(nc.psum_tensor(f"bank{i}", [P, S], F32)) for i in range(8)]

        raw = [sb(f"raw{i}", [P, DC * P]) for i in range(4)]
        whi = [sb(f"whi{i}", [P, DC * P], F32R) for i in range(2)]
        wlo = [sb(f"wlo{i}", [P, DC * P], F32R) for i in range(2)]
        xT = sb("xT", [P, DC, S])
        hhi = sb("hhi", [P, DC, S], F32R)
        hlo = sb("hlo", [P, DC, S], F32R)
        ghi = sb("ghi", [P, DC, S], F32R)
        glo = sb("glo", [P, DC, S], F32R)
        mem_hi = hhi[:, 4:8, :].rearrange("p c (a t) -> p (c a) t", t=MEM)
        mem_lo = hlo[:, 4:8, :].rearrange("p c (a t) -> p (c a) t", t=MEM)

        vec = sb("vec", [P, N_VEC])
        con = sb("con", [P, N_CON])
        level_mask = sb("level_mask", [P, 2 * LEVELS, P], U8)
        mods = sb("mods", [P, N_ADA])
        gscale = sb("gscale", [P, 9 * DC])
        cact = sb("cact", [P, DC])
        zero_col = sb("zero_col", [P, 1])
        eps_col = sb("eps_col", [P, 1])
        neg_b_in = sb("neg_b_in", [P, 36])
        lbs = sb("lbs", [P, 2, 8])
        lbt = sb("lbt", [P, 3, 8])
        neg_sink = sb("neg_sink", [P, N_Q])
        stat = sb("stat", [P, 2, 6, 4])
        acol = sb("acol", [P, 2, NB, 8])

        square = [sb(f"square{i}", [P, S]) for i in range(2)]
        square_sum = sb("square_sum", [P, S])
        rstd = sb("rstd", [P, S])
        normed = [sb(f"normed{i}", [P, S]) for i in range(2)]
        gate_in = [sb(f"gate_in{i}", [P, S]) for i in range(2)]
        opnd = [sb(f"opnd{i}", [P, S]) for i in range(2)]

        WORK = 16100
        work = sb("work", [P, WORK])
        at = [0]

        def place(*shape):
            n = int(np.prod(shape))
            assert at[0] + n <= WORK, (at, n)
            a = work[:, at[0]:at[0] + n]
            at[0] += n
            return a.rearrange("p (a b) -> p a b", b=shape[1]) if len(shape) == 2 else a

        qT = place(DC, S)
        kT = place(2, S)
        v_tok = place(NB, N_KV * HD)
        rope = place(2, S)
        conv_in = [place(S + 2) for _ in range(2)]
        conv_out = place(S)
        merged = place(DC, S)
        prob = [place(4, 2 * P) for _ in range(2)]
        probT = place(2, S)
        rope_a, rope_b = prob[0], prob[1]
        mask_f32 = qT[:, 0:4, :].rearrange("p a b -> p (a b)")[:, 0:2 * LEVELS * P]
        mask_f32 = mask_f32.rearrange("p (a b) -> p a b", b=P)
        at[0] = 0
        hg = [{n: place(S) for n in ("q", "f0", "k0", "f1", "k1", "g", "v")} for _ in range(2)]
        q_fwd = place(S)
        fprod = [place(S) for _ in range(2)]
        scT = place(NB * (S + P))
        ml = [{"q": place(S + 4), "k": place(S + 4), "v": place(S), "o": place(S)} for _ in range(2)]
        gate_rows = place(S)
        assert at[0] <= WORK
        at[0] = 0
        ml_q, ml_k = place(S), place(S)
        neg_m = [place(S) for _ in range(2)]
        em = [place(S) for _ in range(2)]
        dmat = [place(S) for _ in range(2)]
        sT = [place(NB * (NB + 1) // 2 * P) for _ in range(2)]
        ml_h = [place(S) for _ in range(2)]
        assert at[0] <= 14 * S + 4 * S + NB * (S + P)
        at[0] = 7 * S
        row = {n: place(S) for n in ("ig", "z", "t", "lf", "cum0", "cum1", "a")}
        at[0] = 0
        memT = place(DC, MEM)
        xk = place(DC, MEM)
        xv = place(2, D)
        xq = place(DC, S)
        x_prob = [place(4, 2 * P) for _ in range(2)]
        x_probT = place(2, S)
        x_vT = [place(MEM) for _ in range(2)]

        ident = con[:, CON["ident"]:CON["ident"] + P]
        ones = con[:, CON["ones"]:CON["ones"] + P]
        rot = con[:, CON["rot"]:CON["rot"] + P]
        tri = con[:, CON["tri"]:CON["tri"] + 2 * P].rearrange("p (a b) -> p a b", b=P)
        win = con[:, CON["win"]:CON["win"] + 2 * P]
        sel = con[:, CON["sel"]:CON["sel"] + 8 * P].rearrange("p (a b) -> p a b", b=P)

        def vcol(name, i=0, rows=P):
            return vec[0:rows, VEC[name] + i:VEC[name] + i + 1]

        def mod(kind, c):
            return mods[:, kind * DC + c:kind * DC + c + 1]

        SH = {N_FFN1: 0, N_MIX: 3, N_FFN2: 6}

        def shift(n, c):
            return mod(SH[n], c) if n in SH else zero_col[:, 0:1]

        small_in = sem("small_in")
        rope_in_s = sem("rope_landed")
        x_landed = sem("x_landed")
        mem_landed = sem("mem_landed")
        landed = [sem(f"landed{i}") for i in range(4)]
        w_hi = sem("w_hi")
        w_split = sem("w_split")
        unit_done = sem("unit_done")
        evac = [sem(f"evac{i}") for i in range(2)]
        ada_done = sem("ada_done")
        cact_ready = sem("cact_ready")
        setup_v = sem("setup_v")
        setup_a = sem("setup_a")
        mods_done = sem("mods_done")
        sq_done, sq_added, sum_done = sem("sq_done"), sem("sq_added"), sem("sum_done")
        rstd_ln, rstd_done = sem("rstd_ln"), sem("rstd_done")
        normed_done, h_hi, h_ready = sem("normed_done"), sem("h_hi"), sem("h_ready")
        op_src, op_hi, op_ready = sem("op_src"), sem("op_hi"), sem("op_ready")
        rot_done, rope_mul, rope_done = sem("rot_done"), sem("rope_mul"), sem("rope_done")
        vT_done, vtok_done = sem("vT_done"), sem("vtok_done")
        conv_step, pad_done = sem("conv_step"), sem("pad_done")
        score_done, masked, row_max, neg_max = sem("score_done"), sem("masked"), sem("row_max"), sem("neg_max")
        sink_sum, exp_done, den_done, rden_done = sem("sink_sum"), sem("exp_done"), sem("den_done"), sem("rden_done")
        prob_done, turned, turned_out = sem("prob_done"), sem("turned"), sem("turned_out")
        pv_done, pv_out = sem("pv_done"), sem("pv_out")
        gated = sem("gated")
        gate_chain, acol_done = sem("gate_chain"), sem("acol_done")
        sig_done, fk_done = sem("sig_done"), sem("fk_done")
        lev_done, lev_taken, decay = sem("lev_done"), sem("lev_taken"), sem("decay")
        o2_done, hsq_done, hsum_done, hln_done, hrs_done, hnorm_t = (
            sem("o2_done"), sem("hsq_done"), sem("hsum_done"), sem("hln_done"), sem("hrs_done"), sem("hnorm_t"))
        tap_done, qk_done, bc_done, bc_out = sem("tap_done"), sem("qk_done"), sem("bc_done"), sem("bc_out")
        pair_done, d_arg, d_exp, s_mul, s_done = sem("pair_done"), sem("d_arg"), sem("d_exp"), sem("s_mul"), sem("s_done")
        nd_done, abs_done, ml_step = sem("nd_done"), sem("abs_done"), sem("ml_step")
        relu_done = sem("relu_done")
        out_v, stored = sem("out_v"), sem("stored")

        block = ctx.enter_context(nc.Block())

        def x_ready(eng, n, c):
            if n == N_FFN1:
                return eng.wait_ge(x_landed, 16)
            if n == N_MEM:
                return eng.wait_ge(mem_landed, 16)
            if n == N_MIX2:
                return eng.wait_ge(normed_done, DC * N_FINAL + c + 1)
            v = {N_MIX: V_MIX - DC, N_FFN2: V_WO, N_FINAL: V_GATE - DC, N_XATTN: V_WO2, N_MLP: V_XO,
                 N_OUT: V_END - DC}[n] + c
            eng.wait_ge(evac[v % 2], v // 2 + 1)

        def norm_src(n, c):
            return memT[:, c, :] if n == N_MEM else xT[:, c, :]

        def width(n):
            return MEM if n == N_MEM else S

        H_AT = {N_FFN1: 0, N_MIX: 8, N_FFN2: 16, N_MIX2: 24, N_MEM: 32, N_XATTN: 40, N_MLP: 48}

        def h_out(n, c):
            return (mem_hi[:, c, :], mem_lo[:, c, :]) if n == N_MEM else (hhi[:, c, :], hlo[:, c, :])

        def pairs(t, m):
            return t.rearrange("p (j a m) -> p j a m", a=2, m=m)

        def fsrc(s, dr, k):
            if k == 0:
                return s[f"f{dr}"]
            n = S >> k
            return fprod[dr][:, S - 2 * n:S - n]

        diag = scT[:, :].rearrange("p (b c) -> p b c", c=S + P)[:, :, 0:P]

        def slot_units(i):
            return range(V_CONV + 2 * i, V_CONV + 2 * i + 2) if i < 12 else range(V_CP + 4 * (i - 12), V_CP + 4 * (i - 11))

        def s_range(dr, b):
            if dr == 0:
                return b * P, S, sum(S - i * P for i in range(b))
            return 0, (b + 1) * P, sum((i + 1) * P for i in range(b))

        def unit_groups():
            out = []
            for h in range(NH2):
                nxt = range(V_HG + 5 * (h + 1), V_HG + 5 * (h + 2)) if h + 1 < NH2 else range(V_ML, V_ML + 4)
                out.append(("hg", h, list(nxt)))
            for h in range(NH2):
                out.append(("ml", h, list(range(V_ML + 4 * (h + 1), V_ML + 4 * (h + 2))) if h + 1 < NH2 else []))
            return out

        ITEM_SLOTS = [range(0, 4), range(4, 7), range(7, 10), range(10, 14), range(14, ITEMS)]

        @block.sync
        def _(sp):
            sp.dma_start(vec[:], vec_in).then_inc(small_in, 16)
            sp.dma_start(con[:], con_in).then_inc(small_in, 16)
            sp.dma_start(mask_f32, mask_in).then_inc(small_in, 16)

            def load(u, w, kc=DC):
                src = w8_in if kc == DC else w6_in
                sp.dma_start(raw[u % 4][:, 0:kc * P], src[w]).then_inc(landed[u % 4], 16)

            user = {raw_of(v): (w_split, v + 1) for v in range(V_END)}
            user |= {raw_of_ada(a): (ada_done, a + 1) for a in range(N_ADA)}

            def load_at(u, w, kc=DC):
                if u >= 4:
                    sp.wait_ge(*user[u - 4])
                load(u, w, kc)

            for u in range(4):
                load_at(u, u)
            with sp.Fori(1, ADA_FIRST // 4) as i:
                for k in range(4):
                    sp.wait_ge(ada_done, 4 * i + k - 3)
                    load(k, 4 * i + k)
            for part, kc in enumerate(FF_PARTS):
                v0, a0 = 24 * part, ADA_PART[part]
                u0, u1 = raw_of(v0), raw_of(v0 + 2 * kc)
                for u in range(u0, u0 + 8):
                    load_at(u, u)
                with sp.Fori(1, kc // 2) as i:
                    for k in range(4):
                        sp.wait_ge(w_split, v0 + k - 1 + 4 * i)
                        load(u0 + 2 * k, u0 + 2 * k + 8 * i)
                        sp.wait_ge(ada_done, a0 + k - 1 + 4 * i)
                        load(u0 + 2 * k + 1, u0 + 2 * k + 1 + 8 * i)
                for u in range(u0 + 4 * kc, u1):
                    load_at(u, u)
                for c in range(DC):
                    load_at(u1 + c, u1 + c if kc == DC else c, kc)

            def run(v0, v1, w0, kc=DC):
                for k in range(4):
                    load_at(raw_of(v0 + k), w0 + k, kc)
                if v1 - v0 >= 8:
                    with sp.Fori(1, (v1 - v0) // 4) as i:
                        for k in range(4):
                            sp.wait_ge(w_split, v0 + k - 3 + 4 * i)
                            load(raw_of(v0 + k), w0 + k + 4 * i, kc)
                for k in range((v1 - v0) // 4 * 4, v1 - v0):
                    load_at(raw_of(v0 + k), w0 + k, kc)

            down2 = V_FFN[1] + 60
            row0 = raw_of(V_MIX) - DC
            run(V_MIX, down2, row0)
            run(down2, V_GATE, DC, FF_PARTS[2])
            run(V_GATE, V_END, row0 + down2 - V_MIX)
            sp.wait_ge(stored, 16 * DC)

        @block.gpsimd
        def _(pool):
            pool.dma_start(xT[:], x_in).then_inc(x_landed, 16)
            pool.dma_start(rope, rope_in).then_inc(rope_in_s, 16)
            for n in range(9):
                w = width(n)
                if n == N_MEM:
                    pool.wait_ge(op_ready, J_Y2 + DC)
                    pool.dma_start(memT, mem_in).then_inc(mem_landed, 16)
                for c in range(1, DC):
                    pool.wait_ge(sq_done, DC * n + c + 1)
                    if c > 1:
                        pool.wait_ge(sq_added, (DC - 1) * n + c - 1)
                    nc.gpsimd.tensor_tensor(square_sum[:, 0:w], square_sum[:, 0:w], square[c % 2][:, 0:w],
                                            ALU.add).then_inc(sq_added, 1)

        @block.scalar
        def _(act):
            nxt = [0]

            def split(v, dv=0, u=None, du=0):
                kc = chunks_of(v)
                u = raw_of(v) if u is None else u
                act.wait_ge(landed[u % 4], 16 * (u // 4 + 1) + 16 * du)
                if v >= 2 or not isinstance(dv, int):
                    act.wait_ge(unit_done, v - 1 + 4 * dv)
                nc.scalar.activation(whi[v % 2][:, 0:kc * P], raw[u % 4][:, 0:kc * P], ACT.Copy).then_inc(w_hi, 1)

            def split_next(v):
                if nxt[0] <= v + 1 < V_END:
                    split(v + 1)
                    nxt[0] = v + 2

            def norm_stats(n):
                w = width(n)
                for c in range(DC):
                    x_ready(act, n, c)
                    if c == 0 and n > 0:
                        act.wait_ge(sum_done, n)
                    if c > 2:
                        act.wait_ge(sq_added, (DC - 1) * n + c - 2)
                    dst = square_sum if c == 0 else square[c % 2]
                    nc.scalar.activation(dst[:, 0:w], norm_src(n, c), ACT.Square).then_inc(sq_done, 1)
                act.wait_ge(sum_done, n + 1)
                if n > 0:
                    act.wait_ge(normed_done, DC * n)
                nc.scalar.activation(rstd[:, 0:w], bank[4][:, 0:w], ACT.Ln, bias=eps_col[:, 0:1],
                                     scale=1.0 / D).then_inc(rstd_ln, 1)
                act.wait_ge(rstd_ln, n + 1)
                nc.scalar.activation(rstd[:, 0:w], rstd[:, 0:w], ACT.Exp, scale=-0.5).then_inc(rstd_done, 1)

            def norm_hi(n, free=None):
                w = width(n)
                for c in range(DC):
                    act.wait_ge(normed_done, DC * n + c + 1)
                    if free is not None and c == 0:
                        act.wait_ge(unit_done, free)
                    nc.scalar.activation(h_out(n, c)[0], normed[c % 2][:, 0:w], ACT.Identity,
                                         bias=shift(n, c)).then_inc(h_hi, 1)

            def operand_hi(j, c):
                nc.scalar.activation(ghi[:, c, :], opnd[j % 2][:], ACT.Copy).then_inc(op_hi, 1)

            def evacuate(v, out_ap, func, bias=None, scale=1.0, n=S):
                b = bank[v % 2][:, 0:n]
                if bias is None:
                    nc.scalar.activation(out_ap, b, func, scale=scale).then_inc(evac[v % 2], 1)
                else:
                    nc.scalar.activation(out_ap, b, func, bias=bias, scale=scale).then_inc(evac[v % 2], 1)

            def swiglu(f):
                base, j0 = V_FFN[f], J_FFN[f]
                for part, kc in enumerate(FF_PARTS):
                    v0, j1 = base + 24 * part, j0 + 8 * part

                    def body(i, last):
                        ru = 2 if f == 0 else 1
                        for k in range(2):
                            v = v0 + 2 * k
                            split(v + 1, i, raw_of(v + 1), ru * i)
                            act.wait_ge(unit_done, v + 1 + 4 * i)
                            nc.scalar.activation(gate_in[k][:], bank[0][:], ACT.Silu).then_inc(evac[0], 1)
                            if k == 0:
                                split(v + 2, i, raw_of(v + 2), ru * i)
                            elif not last:
                                split(v0, i + 1, raw_of(v0), ru * (i + 1))
                            else:
                                split(v + 2 + 4 * i)
                            act.wait_ge(evac[1], (v + 1) // 2 + 1 + 2 * i)
                            if isinstance(i, int):
                                g = slice(2 * i + k, 2 * i + k + 1)
                            else:
                                g = bass.ds(2 * i + k, 1)
                                act.wait_ge(small_in, 48)
                            nc.scalar.activation(ghi[:, g, :], opnd[k][:].unsqueeze(1), ACT.Copy).then_inc(op_hi, 1)

                    body(0, False)
                    with act.Fori(1, kc // 2 - 1) as i:
                        body(i, False)
                    body(kc // 2 - 1, True)
                    for c in range(DC):
                        split(v0 + 2 * kc + c + 1)
                nxt[0] = base + V_FFN_LEN + 1

            act.wait_ge(small_in, 48)
            nc.scalar.activation(cact[:], vec[:, VEC["c"]:VEC["c"] + DC], ACT.Silu).then_inc(cact_ready, 1)
            act.wait_ge(setup_v, 1)
            nc.scalar.activation(lbt[:, 1, :], lbt[:, 0, :], ACT.Exp).then_inc(setup_a, 1)
            norm_stats(N_FFN1)
            split(0)
            norm_hi(N_FFN1)
            swiglu(0)

            norm_stats(N_MIX)
            norm_hi(N_MIX)
            for j in range(10):
                v = V_MIX + j
                split_next(v)
                act.wait_ge(unit_done, v + 1)
                if j >= 2:
                    act.wait_ge(rope_mul, 2 * (j - 1))
                evacuate(v, gate_in[j % 2][:], ACT.Copy)
            for t in range(2):
                v = V_MIX + 10 + t
                split_next(v)
                act.wait_ge(unit_done, v + 1)
                act.wait_ge(rope_mul, 2 * (9 + t))
                evacuate(v, gate_in[t][:], ACT.Copy)

            def step_exp(i, S_, n_keys_lo, sink):
                act.wait_ge(neg_max, i + 1)
                for hh in range(4):
                    ins = nc.scalar.activation(S_[i % 2][:, hh, n_keys_lo:], S_[i % 2][:, hh, n_keys_lo:], ACT.Exp,
                                               bias=stat[:, i % 2, NEG_MAX, hh:hh + 1],
                                               accum_out=stat[:, i % 2, SUM, hh:hh + 1])
                if sink:
                    act.wait_ge(sink_sum, i + 1)
                    ins = nc.scalar.activation(stat[:, i % 2, SINK, :], stat[:, i % 2, SINK, :], ACT.Exp)
                ins.then_inc(exp_done, 1)

            def step_turned(i, dst, kbs):
                act.wait_ge(turned, i + 1)
                if i > 0:
                    act.wait_ge(pv_done, i)
                for kb in kbs:
                    ins = nc.scalar.activation(dst[:, kb, :], bank[4 + kb][:], ACT.Copy)
                ins.then_inc(turned_out, 1)

            def kbs_of(i):
                return range(0 if i % 4 else 1, 2)

            def conv_unit(v):
                c, k = divmod(v - V_CONV, 3)
                split_next(v)
                if k == 0:
                    act.wait_ge(unit_done, v + 1)
                    if c == 0:
                        act.wait_ge(vT_done, 2)
                    elif c >= 2:
                        vp = V_CONV + 3 * (c - 2) + 1
                        act.wait_ge(evac[vp % 2], vp // 2 + 1)
                    evacuate(v, gate_in[c % 2][:], ACT.Copy)
                if k == 2:
                    act.wait_ge(evac[v % 2], v // 2 + 1)
                    operand_hi(J_Y + c, c)

            def gate_unit(v, base):
                c, k = divmod(v - base, 2)
                split_next(v)
                if k == 0:
                    act.wait_ge(unit_done, v + 1)
                    if v >= V_CP + 4:
                        act.wait_ge(evac[(v - 3) % 2], (v - 3) // 2 + 1)
                    else:
                        vp = V_CONV + 3 * (6 + c) + 1
                        act.wait_ge(evac[vp % 2], vp // 2 + 1)
                    evacuate(v, gate_in[c % 2][:], ACT.Sigmoid)

            for i in range(16):
                units = slot_units(i)
                lo = 0 if i % 4 else P
                if i > 0:
                    step_turned(i - 1, probT, kbs_of(i - 1))
                for a, v in enumerate(units):
                    (conv_unit if v < V_CP else lambda u: gate_unit(u, V_CP))(v)
                    if a == 0:
                        step_exp(i, prob, lo, True)
            step_turned(15, probT, kbs_of(15))
            for c in range(DC):
                act.wait_ge(pv_out, 16)
                if c == 0:
                    act.wait_ge(unit_done, V_AP)
                nc.scalar.activation(ghi[:, c, :], qT[:, c, :], ACT.Copy).then_inc(op_hi, 1)
            for c in range(2 * DC):
                gate_unit(V_AP + c, V_AP)
            for c in range(DC):
                act.wait_ge(gated, DC)
                act.wait_ge(unit_done, V_WO)
                nc.scalar.activation(hhi[:, c, :], merged[:, c, :], ACT.Copy).then_inc(op_hi, 1)
            for c in range(DC):
                split_next(V_WO + c)
            norm_stats(N_FFN2)
            norm_hi(N_FFN2)
            swiglu(1)

            norm_stats(N_FINAL)
            norm_stats(N_MIX2)
            norm_hi(N_MIX2)
            split_next(V_GATE)

            def b_in(i):
                return vcol("b_in", i)

            act.wait_ge(unit_done, V_GATE + 1)
            nc.scalar.activation(row["ig"][0:8, :], bank[V_GATE % 2][0:8, :], ACT.Identity,
                                 bias=vcol("b_gate", 0, 8)).then_inc(evac[V_GATE % 2], 1)
            nc.scalar.activation(row["z"][0:8, :], bank[2][0:8, :], ACT.Identity,
                                 bias=vcol("b_gate", 1, 8)).then_inc(gate_chain, 1)
            act.wait_ge(gate_chain, 1)
            nc.scalar.activation(row["t"][0:8, :], row["z"][0:8, :], ACT.Abs).then_inc(gate_chain, 1)
            act.wait_ge(gate_chain, 2)
            nc.scalar.activation(row["t"][0:8, :], row["t"][0:8, :], ACT.Exp, scale=-1.0).then_inc(gate_chain, 1)
            act.wait_ge(gate_chain, 3)
            nc.scalar.activation(row["t"][0:8, :], row["t"][0:8, :], ACT.Ln, bias=1.0).then_inc(gate_chain, 1)

            def group_unit(v):
                split_next(v)
                if v < V_ML:
                    h, k = divmod(v - V_HG, 5)
                    s = hg[h % 2]
                    col = (0, 4, 8, 12, 16)[k] + h
                    act.wait_ge(unit_done, v + 1)
                    if h >= 2 and k == 0:
                        act.wait_ge(op_ready, J_Y2 + h - 1)
                    if h == 1 and k == 0:
                        act.wait_ge(acol_done, 1)
                    if k == 0:
                        evacuate(v, s["q"], ACT.Silu, bias=b_in(col))
                    elif k in (1, 2):
                        nc.scalar.activation(s[f"f{k - 1}"], bank[v % 2][:], ACT.Sigmoid,
                                             bias=b_in(col)).then_inc(sig_done, 1)
                        evacuate(v, s[f"k{k - 1}"], ACT.Sigmoid, bias=neg_b_in[:, col:col + 1], scale=-1.0)
                    elif k == 3:
                        if h > 0:
                            act.wait_ge(vT_done, 2 + h)
                        evacuate(v, gate_in[0][:], ACT.Identity, bias=b_in(col))
                    else:
                        evacuate(v, s["g"], ACT.Silu, bias=b_in(col))
                else:
                    h, k = divmod(v - V_ML, 4)
                    s = ml[h % 2]
                    col = 20 + 4 * k + h
                    act.wait_ge(unit_done, v + 1)
                    if h == 0 and k == 0:
                        act.wait_ge(pad_done, 3)
                    if h >= 2 and k == 0:
                        act.wait_ge(op_ready, J_Y2 + 4 + h - 1)
                    if k < 2:
                        evacuate(v, s["qk"[k]][:, 2:2 + S], ACT.Identity, bias=b_in(col))
                    elif k == 2:
                        act.wait_ge(vT_done, 2 + NH2 + h)
                        evacuate(v, gate_in[0][:], ACT.Identity, bias=b_in(col))
                    else:
                        evacuate(v, s["o"], ACT.Sigmoid, bias=b_in(col))

            def head_norm(h, src):
                nc.scalar.activation(square[0][:], src, ACT.Square).then_inc(hsq_done, 1)
                act.wait_ge(hsum_done, h + 1)
                nc.scalar.activation(rstd[:], bank[4][:], ACT.Ln, bias=eps_col[:, 0:1], scale=1.0 / P).then_inc(hln_done, 1)
                act.wait_ge(hln_done, h + 1)
                nc.scalar.activation(rstd[:], rstd[:], ACT.Exp, scale=-0.5).then_inc(hrs_done, 1)
                act.wait_ge(op_src, h + 1)
                nc.scalar.activation(ghi[:, h, :], opnd[h % 2][:], ACT.Copy).then_inc(op_hi, 1)

            for k in range(5):
                group_unit(V_HG + k)
            for kind, h, units in unit_groups():
                if kind == "hg":
                    for v in units:
                        group_unit(v)
                    act.wait_ge(o2_done, h + 1)
                    head_norm(h, bank[6][:])
                    continue
                units = list(units)
                for k in range(4):
                    act.wait_ge(bc_done, 4 * h + k + 1)
                    dst, func = (neg_m[k], ACT.Copy) if k < 2 else (em[k - 2], ACT.Exp)
                    if h > 0 and k == 0:
                        act.wait_ge(ml_step, ML_STEPS * h)
                    nc.scalar.activation(dst, bank[5][:], func).then_inc(bc_out, 1)
                for k in range(2):
                    act.wait_ge(tap_done, 10 * h + 5 * k + 5)
                    nc.scalar.activation((ml_q, ml_k)[k], dmat[k], ACT.Silu,
                                         bias=vcol("mconv_b", 4 * k + h)).then_inc(qk_done, 1)
                for y in range(2 * NB):
                    b, dr = divmod(y, 2)
                    t0, t1, _ = s_range(dr, b)
                    act.wait_ge(d_arg, 8 * h + y + 1)
                    nc.scalar.activation(dmat[dr][:, t0:t1], dmat[dr][:, t0:t1], ACT.Exp).then_inc(d_exp, 1)
                    if y % 2 == 1 and units:
                        group_unit(units.pop(0))
                for dr in range(2):
                    act.wait_ge(nd_done, 2 * h + dr + 1)
                    nc.scalar.activation(dmat[dr], bank[(5, 3)[dr]][:], ACT.Abs).then_inc(abs_done, 1)
                act.wait_ge(ml_step, ML_STEPS * (h + 1))
                head_norm(NH2 + h, ml_h[0])

            for c in range(DC):
                split_next(V_WO2 + c)
            norm_stats(N_MEM)
            norm_hi(N_MEM, V_WO2)
            for c in range(DC):
                v = V_XK + c
                split_next(v)
                act.wait_ge(unit_done, v + 1)
                evacuate(v, xk[:, c, :], ACT.Copy, n=MEM)
            for c in range(DC):
                v = V_XV + c
                split_next(v)
                act.wait_ge(unit_done, v + 1)
                if c >= 2:
                    act.wait_ge(vT_done, 10 + c - 1)
                evacuate(v, x_vT[c % 2], ACT.Copy, n=MEM)
            norm_stats(N_XATTN)
            norm_hi(N_XATTN, V_XQ)
            for c in range(DC):
                v = V_XQ + c
                split_next(v)
                act.wait_ge(unit_done, v + 1)
                evacuate(v, xq[:, c, :], ACT.Copy)
            for n in range(NB):
                step_exp(16 + n, x_prob, 0, False)
                step_turned(16 + n, x_probT, range(2))
            for c in range(DC):
                act.wait_ge(pv_out, 20)
                nc.scalar.activation(ghi[:, c, :], xq[:, c, :], ACT.Copy).then_inc(op_hi, 1)
            for c in range(DC):
                split_next(V_XO + c)
            norm_stats(N_MLP)
            norm_hi(N_MLP)

            def mlp(i, last):
                for c in range(DC):
                    v = V_MLP + c
                    split(v + 1, 4 * i, raw_of(v + 1), 4 * i)
                    act.wait_ge(unit_done, v + 1 + 16 * i)
                    nc.scalar.activation(gate_in[c % 2][:], bank[v % 2][:], ACT.Relu).then_inc(evac[v % 2], 1)
                    act.wait_ge(op_src, 8 + c + 1 + DC * i)
                    nc.scalar.activation(ghi[:, c, :], opnd[c % 2][:], ACT.Copy).then_inc(op_hi, 1)
                for c in range(DC):
                    v = V_MLP + DC + c
                    if c < DC - 1 or not last:
                        split(v + 1, 4 * i, raw_of(v + 1), 4 * i)

            with act.Fori(0, MLP_PARTS - 1) as i:
                mlp(i, False)
            mlp(MLP_PARTS - 1, True)
            norm_stats(N_OUT)
            for c in range(DC):
                act.wait_ge(normed_done, DC * N_OUT + c + 1)
                act.dma_start(out[:, c, :], xT[:, c, :]).then_inc(stored, 16)

        @block.vector
        def _(dve):
            nxt = [0]

            def split(v, dv=0):
                kc = chunks_of(v)
                u = raw_of(v)
                dve.wait_ge(w_hi, v + 1 + 4 * dv)
                nc.vector.tensor_tensor(wlo[v % 2][:, 0:kc * P], raw[u % 4][:, 0:kc * P],
                                        whi[v % 2][:, 0:kc * P].bitcast(F32), ALU.subtract).then_inc(w_split, 1)

            def split_next(v):
                if nxt[0] <= v + 1 < V_END:
                    split(v + 1)
                    nxt[0] = v + 2

            def stt(out_ap, in0, scalar, in1, op0, op1):
                return nc.vector.scalar_tensor_tensor(out=out_ap, in0=in0, scalar=scalar, in1=in1, op0=op0, op1=op1)

            def norm(n):
                w = width(n)
                dve.wait_ge(rstd_done, n + 1)

                def rest(c):
                    dve.wait_ge(h_hi, H_AT[n] + c + 1)
                    hi, lo = h_out(n, c)
                    stt(lo, normed[c % 2][:, 0:w], shift(n, c), hi.bitcast(F32), ALU.add,
                        ALU.subtract).then_inc(h_ready, 1)

                for c in range(DC):
                    if n in H_AT:
                        if c >= 2:
                            rest(c - 2)
                        if H_AT[n] + c >= 2:
                            dve.wait_ge(h_ready, H_AT[n] + max(c - 1, 0))
                        dst = normed[c % 2][:, 0:w]
                    else:
                        dst = xT[:, c, :]
                    stt(dst, norm_src(n, c), gscale[:, n * DC + c:n * DC + c + 1], rstd[:, 0:w], ALU.mult,
                        ALU.mult).then_inc(normed_done, 1)
                if n in H_AT:
                    rest(DC - 2)
                    rest(DC - 1)

            def operand_lo(j, c, src=None, bufs=None):
                hi, lo = bufs or (ghi, glo)
                dve.wait_ge(op_hi, j + 1)
                nc.vector.tensor_tensor(lo[:, c, :], opnd[j % 2][:] if src is None else src,
                                        hi[:, c, :].bitcast(F32), ALU.subtract).then_inc(op_ready, 1)

            def residual(v, c, scale=None, dv=0):
                dve.wait_ge(unit_done, v + 1 + 4 * dv)
                if scale is None:
                    ins = nc.vector.tensor_tensor(xT[:, c, :], bank[v % 2][:], xT[:, c, :], ALU.add)
                else:
                    ins = stt(xT[:, c, :], bank[v % 2][:], scale, xT[:, c, :], ALU.mult, ALU.add)
                ins.then_inc(evac[v % 2], 1)

            def swiglu(f):
                base, j0 = V_FFN[f], J_FFN[f]
                for part, kc in enumerate(FF_PARTS):
                    v0, j1 = base + 24 * part, j0 + 8 * part

                    def body(i, last):
                        for k in range(2):
                            v, j = v0 + 2 * k, j1 + k
                            split(v + 1, i)
                            if k == 0:
                                split(v + 2, i)
                            elif not last:
                                split(v0, i + 1)
                            else:
                                split(v + 2 + 4 * i)
                            dve.wait_ge(evac[0], v // 2 + 1 + 2 * i)
                            dve.wait_ge(unit_done, v + 2 + 4 * i)
                            if j >= 2 or not isinstance(i, int) or i > 0:
                                dve.wait_ge(op_ready, j - 1 + 2 * i)
                            nc.vector.tensor_tensor(opnd[k][:], bank[1][:], gate_in[k][:], ALU.mult).then_inc(evac[1], 1)
                            dve.wait_ge(op_hi, j + 1 + 2 * i)
                            if isinstance(i, int):
                                g = slice(2 * i + k, 2 * i + k + 1)
                            else:
                                g = bass.ds(2 * i + k, 1)
                            nc.vector.tensor_tensor(glo[:, g, :], opnd[k][:].unsqueeze(1), ghi[:, g, :].bitcast(F32),
                                                    ALU.subtract).then_inc(op_ready, 1)

                    body(0, False)
                    with dve.Fori(1, kc // 2 - 1) as i:
                        body(i, False)
                    body(kc // 2 - 1, True)
                    if f == 0 and part == 0:
                        dve.wait_ge(ada_done, ADA_FIRST)
                        nc.vector.tensor_tensor(mods[:, 2 * DC:3 * DC], bank[5][:, 0:DC],
                                                vec[:, VEC["b_ada"] + 2 * DC:VEC["b_ada"] + 3 * DC], ALU.add).then_inc(mods_done, 1)
                        dve.wait_ge(mods_done, 4)
                        nc.vector.tensor_scalar(mods[:, 2 * DC:3 * DC], mods[:, 2 * DC:3 * DC], 0.5, None,
                                                ALU.mult).then_inc(mods_done, 1)
                        dve.wait_ge(mods_done, 5)
                    v = v0 + 2 * kc
                    for c in range(DC):
                        split(v + c + 1)
                        residual(v + c, c, mod(2 if f == 0 else 8, c))
                nxt[0] = base + V_FFN_LEN + 1

            for t, val in ((zero_col, 0.0), (eps_col, EPS)):
                nc.vector.memset(t[:], val)
            dve.wait_ge(small_in, 48)
            nc.vector.tensor_copy(level_mask[:], mask_f32)
            lbv = vec[:, VEC["lb"]:VEC["lb"] + 8]
            nc.vector.tensor_tensor(lbt[:, 0, :], lbv, lbv, ALU.subtract).then_inc(setup_v, 1)
            nc.vector.tensor_scalar(neg_b_in[:], vec[:, VEC["b_in"]:VEC["b_in"] + 36], -1.0, None, ALU.mult)
            nc.vector.tensor_scalar(neg_sink[:], vec[:, VEC["sinks"]:VEC["sinks"] + N_Q], -1.0, None,
                                    ALU.mult).then_inc(setup_v, 1)
            dve.wait_ge(setup_a, 1)
            nc.vector.reciprocal(lbt[:, 2, :], lbt[:, 1, :]).then_inc(setup_v, 1)
            dve.wait_ge(setup_v, 3)
            nc.vector.tensor_tensor(lbt[:, 0, :], lbt[:, 1, :], lbt[:, 2, :], ALU.mult).then_inc(setup_v, 1)
            dve.wait_ge(setup_v, 4)
            nc.vector.tensor_tensor(lbs[:, 0, :], lbt[:, 0, :], lbt[:, 0, :], ALU.subtract).then_inc(setup_v, 1)
            dve.wait_ge(setup_v, 5)
            nc.vector.tensor_scalar(lbs[:, 1, :], lbs[:, 0, :], -1.0, 1.0, ALU.mult, ALU.add).then_inc(setup_v, 1)
            gain = vec[:, VEC["gain"]:VEC["gain"] + 9 * DC]
            nc.vector.tensor_copy(gscale[:], gain).then_inc(mods_done, 1)
            dve.wait_ge(ada_done, ADA_HEAD_N)
            nc.vector.tensor_tensor(mods[:, 0:16], bank[6][:, 0:16], vec[:, VEC["b_ada"]:VEC["b_ada"] + 16],
                                    ALU.add).then_inc(mods_done, 1)
            dve.wait_ge(mods_done, 2)
            stt(gscale[:, 0:DC], mods[:, DC:2 * DC], 1.0, gain[:, 0:DC], ALU.add, ALU.mult).then_inc(mods_done, 1)
            dve.wait_ge(mods_done, 3)
            norm(N_FFN1)
            split(0)
            swiglu(0)
            dve.wait_ge(ada_done, N_ADA)
            nc.vector.tensor_tensor(mods[:, 24:N_ADA], bank[7][:, 24:N_ADA], vec[:, VEC["b_ada"] + 24:VEC["b_ada"] + N_ADA],
                                    ALU.add).then_inc(mods_done, 1)
            dve.wait_ge(mods_done, 6)
            for n in (N_MIX, N_FFN2):
                k = SH[n] + 1
                stt(gscale[:, n * DC:(n + 1) * DC], mods[:, k * DC:(k + 1) * DC], 1.0, gain[:, n * DC:(n + 1) * DC],
                    ALU.add, ALU.mult).then_inc(mods_done, 1)
            nc.vector.tensor_scalar(mods[:, 8 * DC:], mods[:, 8 * DC:], 0.5, None, ALU.mult).then_inc(mods_done, 1)
            dve.wait_ge(mods_done, 9)

            norm(N_MIX)
            for i in range(2):
                nc.vector.memset(conv_in[i][:, 0:2], 0.0).then_inc(pad_done, 1)
            dve.wait_ge(rope_in_s, 16)
            for j in range(10):
                v = V_MIX + j
                split_next(v)
                ra, rb = rope_a[:, 0:2, :].rearrange("p a b -> p (a b)"), rope_b[:, 0:2, :].rearrange("p a b -> p (a b)")
                dve.wait_ge(evac[v % 2], v // 2 + 1)
                if j > 0:
                    dve.wait_ge(rope_done, j)
                nc.vector.tensor_tensor(ra, gate_in[j % 2][:], rope[:, 0, :], ALU.mult).then_inc(rope_mul, 1)
                dve.wait_ge(rot_done, j + 1)
                nc.vector.tensor_tensor(rb, bank[2 + j % 2][:], rope[:, 1, :], ALU.mult).then_inc(rope_mul, 1)
                dve.wait_ge(rope_mul, 2 * j + 2)
                dst = qT[:, j, :] if j < DC else kT[:, j - DC, :]
                nc.vector.tensor_tensor(dst, ra, rb, ALU.add).then_inc(rope_done, 1)
            for t in range(2):
                split_next(V_MIX + 10 + t)
                dve.wait_ge(vT_done, t + 1)
                nc.vector.tensor_copy(v_tok[:, :, t * P:(t + 1) * P],
                                      bank[4 + t][:].rearrange("p (a b) -> p a b", b=P)).then_inc(vtok_done, 1)

            def softmax_first(i, S_, lo, sink, scale):
                p = i % 2
                dve.wait_ge(score_done, i + 1)
                if i == 0:
                    dve.wait_ge(rope_done, 10)
                if i >= 2:
                    dve.wait_ge(turned, i - 1)
                for a in range(2):
                    src = bank[2 + a][:].rearrange("p (h k) -> p h k", k=2 * P)[:, :, lo:]
                    dst = S_[p][:, 2 * a:2 * a + 2, lo:]
                    if sink:
                        mask = win[:, lo:].unsqueeze(1).to_broadcast([P, 2, 2 * P - lo])
                        stt(dst, src, scale, mask, ALU.mult, ALU.add).then_inc(masked, 1)
                    else:
                        nc.vector.tensor_scalar(dst, src, scale, None, ALU.mult).then_inc(masked, 1)
                dve.wait_ge(masked, 2 * i + 2)
                nc.vector.tensor_reduce(stat[:, p, ROW_MAX, :], S_[p][:, :, lo:], AX_X, ALU.max).then_inc(row_max, 1)
                dve.wait_ge(row_max, i + 1)
                if sink:
                    g = i // 4
                    stt(stat[:, p, NEG_MAX, :], stat[:, p, ROW_MAX, :], -1.0, neg_sink[:, 4 * g:4 * g + 4], ALU.mult,
                        ALU.min).then_inc(neg_max, 1)
                    dve.wait_ge(neg_max, i + 1)
                    nc.vector.tensor_tensor(stat[:, p, SINK, :], stat[:, p, NEG_MAX, :],
                                            vec[:, VEC["sinks"] + 4 * g:VEC["sinks"] + 4 * g + 4],
                                            ALU.add).then_inc(sink_sum, 1)
                else:
                    nc.vector.tensor_scalar(stat[:, p, NEG_MAX, :], stat[:, p, ROW_MAX, :], -1.0, None,
                                            ALU.mult).then_inc(neg_max, 1)

            def softmax_last(i, S_, lo, sink):
                p = i % 2
                dve.wait_ge(exp_done, i + 1)
                den = stat[:, p, SUM, :]
                if sink:
                    nc.vector.tensor_tensor(stat[:, p, DEN, :], den, stat[:, p, SINK, :], ALU.add).then_inc(den_done, 1)
                    dve.wait_ge(den_done, i + 1)
                    den = stat[:, p, DEN, :]
                nc.vector.reciprocal(stat[:, p, RDEN, :], den).then_inc(rden_done, 1)
                dve.wait_ge(rden_done, i + 1)
                for hh in range(4):
                    ins = nc.vector.tensor_scalar(S_[p][:, hh, lo:], S_[p][:, hh, lo:], stat[:, p, RDEN, hh:hh + 1], None,
                                                  ALU.mult)
                ins.then_inc(prob_done, 1)

            def take_output(i):
                g, n = divmod(i, 4)
                half = (g % 2) * HD
                dve.wait_ge(pv_done, i + 1)
                nc.vector.tensor_copy(qT[half:half + HD, 4 * (g // 2):4 * (g // 2) + 4, n * P:(n + 1) * P],
                                      bank[6][0:HD, :].rearrange("p (h q) -> p h q", q=P)).then_inc(pv_out, 1)

            def conv_unit(v):
                c, k = divmod(v - V_CONV, 3)
                split_next(v)
                cin = conv_in[c % 2]
                if k == 1:
                    dve.wait_ge(evac[(v - 1) % 2], (v - 1) // 2 + 1)
                    dve.wait_ge(unit_done, v + 1)
                    nc.vector.tensor_tensor(cin[:, 2:], bank[v % 2][:], gate_in[c % 2][:], ALU.mult).then_inc(evac[v % 2], 1)
                    dve.wait_ge(evac[v % 2], v // 2 + 1)
                    for tap in range(3):
                        src = cin[:, 2 - tap:2 - tap + S]
                        w = vcol("conv_w", DC * (2 - tap) + c)
                        if tap == 0:
                            ins = nc.vector.tensor_scalar(conv_out, src, w, None, ALU.mult)
                        else:
                            dve.wait_ge(conv_step, 3 * c + tap)
                            ins = stt(conv_out, src, w, conv_out, ALU.mult, ALU.add)
                        ins.then_inc(conv_step, 1)
                if k == 2:
                    dve.wait_ge(unit_done, v + 1)
                    dve.wait_ge(conv_step, 3 * c + 3)
                    dve.wait_ge(op_ready, J_Y + c - 1)
                    nc.vector.tensor_tensor(opnd[c % 2][:], bank[v % 2][:], conv_out, ALU.mult).then_inc(evac[v % 2], 1)
                    operand_lo(J_Y + c, c)

            def gate_unit(v, base):
                c, k = divmod(v - base, 2)
                split_next(v)
                if k == 1:
                    dve.wait_ge(evac[(v - 1) % 2], (v - 1) // 2 + 1)
                    dve.wait_ge(unit_done, v + 1)
                    if base == V_CP:
                        nc.vector.tensor_tensor(merged[:, c, :], bank[v % 2][:], gate_in[c % 2][:],
                                                ALU.mult).then_inc(evac[v % 2], 1)
                    else:
                        nc.vector.tensor_tensor(conv_out, bank[v % 2][:], gate_in[c % 2][:],
                                                ALU.mult).then_inc(evac[v % 2], 1)
                        dve.wait_ge(evac[v % 2], v // 2 + 1)
                        nc.vector.tensor_tensor(merged[:, c, :], merged[:, c, :], conv_out, ALU.add).then_inc(gated, 1)

            for i in range(16):
                units = slot_units(i)
                lo = 0 if i % 4 else P
                for a, v in enumerate(units):
                    (conv_unit if v < V_CP else lambda u: gate_unit(u, V_CP))(v)
                    if a == 0:
                        softmax_first(i, prob, lo, True, SCORE_SCALE)
                        if i > 0:
                            take_output(i - 1)
                softmax_last(i, prob, lo, True)
            take_output(15)
            for c in range(DC):
                if c == 0:
                    dve.wait_ge(pv_out, 16)
                operand_lo(J_O + c, c, src=qT[:, c, :])
            for c in range(2 * DC):
                gate_unit(V_AP + c, V_AP)
            for c in range(DC):
                operand_lo(J_M + c, c, src=merged[:, c, :], bufs=(hhi, hlo))
            for c in range(DC):
                split_next(V_WO + c)
                residual(V_WO + c, c, mod(5, c))
            norm(N_FFN2)
            swiglu(1)

            norm(N_FINAL)
            norm(N_MIX2)
            split_next(V_GATE)
            for dr in range(2):
                for t in "qk":
                    for cols in (slice(0, 2), slice(S + 2, S + 4)):
                        ins = nc.vector.memset(ml[dr][t][:, cols], 0.0)
            ins.then_inc(pad_done, 1)
            dve.wait_ge(gate_chain, 4)
            dve.wait_ge(evac[V_GATE % 2], V_GATE // 2 + 1)
            R = {k: t[0:8, :] for k, t in row.items()}
            chain = [4]

            def link(ins):
                chain[0] += 1
                ins.then_inc(gate_chain, 1)
                dve.wait_ge(gate_chain, chain[0])

            link(stt(R["lf"], R["z"], 0.0, R["t"], ALU.min, ALU.subtract))
            for dr in range(2):
                rev = (lambda t: t) if dr == 0 else (lambda t: t[:, ::-1])
                a_row = R["a"] if dr == 0 else R["z"]
                link(nc.vector.tensor_tensor_scan(rev(R[f"cum{dr}"]), rev(R["lf"]), rev(R["lf"]), 0.0, ALU.add, ALU.bypass))
                link(nc.vector.tensor_tensor(a_row, R["ig"], R[f"cum{dr}"], ALU.subtract))
                link(nc.vector.tensor_tensor_scan(rev(R["t"]), rev(a_row), rev(a_row), 0.0, ALU.max, ALU.max))
                nc.vector.tensor_scalar(gate_rows[32 * dr:32 * dr + 8, :], R["t"], -1.0, None, ALU.mult)
                link(stt(gate_rows[64 + 32 * dr:72 + 32 * dr, :], R["t"], -1.0, R[f"cum{dr}"], ALU.mult, ALU.subtract))

            def group_unit(v):
                split_next(v)
                if v < V_ML:
                    h, k = divmod(v - V_HG, 5)
                    s = hg[h % 2]
                    if k in (1, 2):
                        d = k - 1
                        col = 4 * d + h
                        dve.wait_ge(sig_done, 2 * h + d + 1)
                        nc.vector.tensor_scalar(s[f"f{d}"], s[f"f{d}"], lbs[:, 1, col:col + 1], lbs[:, 0, col:col + 1],
                                                ALU.mult, ALU.add).then_inc(fk_done, 1)
                        dve.wait_ge(evac[v % 2], v // 2 + 1)
                        nc.vector.tensor_scalar(s[f"k{d}"], s[f"k{d}"], lbs[:, 1, col:col + 1], None,
                                                ALU.mult).then_inc(fk_done, 1)
                    if k == 3:
                        dve.wait_ge(vT_done, 2 + h + 1)
                        nc.vector.tensor_copy(s["v"], bank[5][:]).then_inc(vtok_done, 1)
                else:
                    h, k = divmod(v - V_ML, 4)
                    if k == 2:
                        dve.wait_ge(vT_done, 2 + NH2 + h + 1)
                        nc.vector.tensor_copy(ml[h % 2]["v"], bank[4][:]).then_inc(vtok_done, 1)

            def head_out(h, src, gname, gate):
                dve.wait_ge(hrs_done, h + 1)
                stt(normed[0][:], src, vcol(gname, h % NH2), rstd[:], ALU.mult, ALU.mult).then_inc(hnorm_t, 1)
                dve.wait_ge(hnorm_t, h + 1)
                nc.vector.tensor_tensor(opnd[h % 2][:], normed[0][:], gate, ALU.mult).then_inc(op_src, 1)
                operand_lo(J_Y2 + h, h)

            def update(h, s, m, dr):
                f = fsrc(s, dr, m)
                fp = f.rearrange("p (j a) -> p j a", a=2)
                n, blk = S >> (m + 1), 1 << m
                qq = pairs(q_fwd if dr == 0 else s["q"], blk)
                kk = pairs(s[f"k{dr}"], blk)
                late = 1 - dr
                if m < LEVELS:
                    nc.vector.tensor_tensor(fsrc(s, dr, m + 1).unsqueeze(2), fp[:, :, 0:1], fp[:, :, 1:2], ALU.mult)
                nc.vector.tensor_tensor(qq[:, :, late, :], qq[:, :, late, :],
                                        fp[:, :, 1 - late:2 - late].to_broadcast([P, n, blk]), ALU.mult)
                nc.vector.tensor_tensor(kk[:, :, 1 - late, :], kk[:, :, 1 - late, :],
                                        fp[:, :, late:late + 1].to_broadcast([P, n, blk]), ALU.mult).then_inc(decay, 1)

            def hg_items(h, zs):
                s = hg[h % 2]
                for z in zs:
                    dve.wait_ge(lev_done, ITEMS * h + z + 1)
                    b = bank[2 + z % 2][:]
                    b3 = b.rearrange("p (a t) -> p a t", t=P)
                    if z == 0:
                        nc.vector.tensor_tensor(diag, b3, ident.unsqueeze(1).to_broadcast([P, NB, P]),
                                                ALU.mult).then_inc(lev_taken, 1)
                        dve.wait_ge(fk_done, 4 * h + 4)
                        nc.vector.tensor_tensor(s["q"], s["q"], s["f1"], ALU.mult).then_inc(decay, 1)
                    elif z <= 2 * LEVELS:
                        m, dr = divmod(z - 1, 2)
                        dve.wait_ge(lev_taken, ITEMS * h + z)
                        nc.vector.copy_predicated(diag, level_mask[:, 2 * m + dr, :].unsqueeze(1).to_broadcast([P, NB, P]),
                                                  b3).then_inc(lev_taken, 1)
                        dve.wait_ge(decay, EVENTS * h + (2 + dr if m == 0 else 4 + dr + 2 * (m - 1)))
                        update(h, s, m, dr)
                    elif z == 2 * LEVELS + 1:
                        for k, (sb_, tb) in enumerate(((0, 1), (2, 3), (1, 0), (3, 2))):
                            ins = nc.vector.tensor_copy(scT[:, sb_ * S + tb * P:sb_ * S + (tb + 1) * P], b3[:, k, :])
                        ins.then_inc(lev_taken, 1)
                        for dr in range(2):
                            dve.wait_ge(decay, EVENTS * h + 4 + dr + 2 * (LEVELS - 1))
                            update(h, s, LEVELS, dr)
                    else:
                        dr = z - 2 * LEVELS - 2
                        for k in range(2):
                            sb_ = (0, 2)[dr] + k
                            t0 = (S // 2, 0)[dr]
                            ins = nc.vector.tensor_copy(scT[:, sb_ * S + t0:sb_ * S + t0 + S // 2],
                                                        b[:, k * S // 2:(k + 1) * S // 2])
                        ins.then_inc(lev_taken, 1)

            for k in range(5):
                group_unit(V_HG + k)
            dve.wait_ge(acol_done, 1)
            nc.vector.tensor_copy(acol[:].rearrange("p a b c -> p (a b c)"), bank[3][:, 0:64]).then_inc(acol_done, 1)
            for kind, h, units in unit_groups():
                units = list(units)
                if kind == "hg":
                    s = hg[h % 2]
                    vq = V_HG + 5 * h
                    dve.wait_ge(evac[vq % 2], vq // 2 + 1)
                    dve.wait_ge(fk_done, 4 * h + 4)
                    nc.vector.tensor_tensor(normed[1][:], s["k0"], s["k1"], ALU.add).then_inc(decay, 1)
                    if h > 0:
                        dve.wait_ge(lev_done, ITEMS * h)
                    nc.vector.tensor_tensor(q_fwd, s["q"], s["f0"], ALU.mult).then_inc(decay, 1)
                    for sl in range(5):
                        if units:
                            group_unit(units.pop(0))
                        if sl == 0 and h > 0:
                            dve.wait_ge(o2_done, h)
                        hg_items(h, ITEM_SLOTS[sl])
                    vg = vq + 4
                    dve.wait_ge(evac[vg % 2], vg // 2 + 1)
                    dve.wait_ge(o2_done, h + 1)
                    head_out(h, bank[6][:], "hgrn_g", s["g"])
                    continue
                s = ml[h % 2]
                for k, t in enumerate("qk"):
                    v = V_ML + 4 * h + k
                    dve.wait_ge(evac[v % 2], v // 2 + 1)
                    if h > 0:
                        dve.wait_ge(abs_done, 2 * h)
                    else:
                        dve.wait_ge(op_ready, J_Y2 + NH2)
                    for tap in range(5):
                        w = vcol("mconv_w", DC * tap + 4 * k + h)
                        src = s[t][:, tap:tap + S]
                        if tap == 0:
                            ins = nc.vector.tensor_scalar(dmat[k], src, w, None, ALU.mult)
                        else:
                            dve.wait_ge(tap_done, 10 * h + 5 * k + tap)
                            ins = stt(dmat[k], src, w, dmat[k], ALU.mult, ALU.add)
                        ins.then_inc(tap_done, 1)

                def arg(y):
                    b, dr = divmod(y, 2)
                    t0, t1, _ = s_range(dr, b)
                    if y >= 2:
                        dve.wait_ge(s_mul, 8 * h + y - 1)
                    nc.vector.tensor_scalar(dmat[dr][:, t0:t1], neg_m[dr][:, t0:t1], acol[:, dr, b, 4 * dr + h:4 * dr + h + 1],
                                            0.0, ALU.add, ALU.min).then_inc(d_arg, 1)

                dve.wait_ge(qk_done, 2 * h + 2)
                dve.wait_ge(bc_out, 4 * h + 2)
                if h == 0:
                    dve.wait_ge(acol_done, 2)
                else:
                    dve.wait_ge(nd_done, 2 * h)
                arg(0)
                for y in range(2 * NB):
                    b, dr = divmod(y, 2)
                    t0, t1, at_ = s_range(dr, b)
                    if y + 1 < 2 * NB:
                        arg(y + 1)
                    dve.wait_ge(pair_done, NB * h + b + 1)
                    dve.wait_ge(d_exp, 8 * h + y + 1)
                    stt(sT[dr][:, at_:at_ + t1 - t0], bank[2 + b % 2][:, t0:t1], MLSTM_SCALE, dmat[dr][:, t0:t1],
                        ALU.mult, ALU.mult).then_inc(s_mul, 1)
                    dve.wait_ge(s_mul, 8 * h + y + 1)
                    d = at_ + b * P - t0
                    nc.vector.tensor_tensor(sT[dr][:, d:d + P], sT[dr][:, d:d + P], tri[:, dr, :], ALU.mult).then_inc(s_done, 1)
                    if y % 2 == 1 and units:
                        group_unit(units.pop(0))
                n_ = [ML_STEPS * h]

                def step(ins):
                    n_[0] += 1
                    ins.then_inc(ml_step, 1)
                    dve.wait_ge(ml_step, n_[0])

                for dr in range(2):
                    dve.wait_ge(abs_done, 2 * h + dr + 1)
                    dve.wait_ge(bc_out, 4 * h + 3 + dr)
                    step(nc.vector.tensor_tensor(dmat[dr], dmat[dr], em[dr], ALU.max))
                    step(nc.vector.reciprocal(ml_h[dr], dmat[dr]))
                    step(nc.vector.tensor_tensor(ml_h[dr], bank[6 + dr][:], ml_h[dr], ALU.mult))
                step(nc.vector.tensor_tensor(ml_h[0], ml_h[0], ml_h[1], ALU.add))
                vo = V_ML + 4 * h + 3
                dve.wait_ge(evac[vo % 2], vo // 2 + 1)
                head_out(NH2 + h, ml_h[0], "mlstm_g", s["o"])

            for c in range(DC):
                split_next(V_WO2 + c)
                residual(V_WO2 + c, c)
            norm(N_MEM)
            for c in range(DC):
                split_next(V_XK + c)
            for c in range(DC):
                split_next(V_XV + c)
                dve.wait_ge(vT_done, 10 + c + 1)
                nc.vector.tensor_copy(xv[:, :, c * P:(c + 1) * P],
                                      bank[6 + c % 2][:, 0:MEM].rearrange("p (a b) -> p a b", b=P)).then_inc(vtok_done, 1)
            norm(N_XATTN)
            for c in range(DC):
                split_next(V_XQ + c)
            for n in range(NB):
                i = 16 + n
                softmax_first(i, x_prob, 0, False, XATTN_SCALE)
                softmax_last(i, x_prob, 0, False)
                dve.wait_ge(pv_done, i + 1)
                for a in range(2):
                    ins = nc.vector.tensor_copy(xq[:, 4 * a:4 * a + 4, n * P:(n + 1) * P],
                                                bank[6 + a][:].rearrange("p (h q) -> p h q", q=P))
                ins.then_inc(pv_out, 1)
            for c in range(DC):
                if c == 0:
                    dve.wait_ge(pv_out, 20)
                operand_lo(J_XO + c, c, src=xq[:, c, :])
            for c in range(DC):
                split_next(V_XO + c)
                residual(V_XO + c, c)
            norm(N_MLP)

            def mlp(i, last):
                for c in range(DC):
                    v = V_MLP + c
                    split(v + 1, 4 * i)
                    dve.wait_ge(evac[v % 2], v // 2 + 1 + 8 * i)
                    dve.wait_ge(op_ready, J_MLP + c - 1 + DC * i)
                    nc.vector.tensor_tensor(opnd[c % 2][:], gate_in[c % 2][:], gate_in[c % 2][:], ALU.mult).then_inc(op_src, 1)
                    dve.wait_ge(op_hi, J_MLP + c + 1 + DC * i)
                    nc.vector.tensor_tensor(glo[:, c, :], opnd[c % 2][:], ghi[:, c, :].bitcast(F32),
                                            ALU.subtract).then_inc(op_ready, 1)
                for c in range(DC):
                    v = V_MLP + DC + c
                    if c < DC - 1 or not last:
                        split(v + 1, 4 * i)
                    residual(v, c, dv=4 * i)

            with dve.Fori(0, MLP_PARTS - 1) as i:
                mlp(i, False)
            mlp(MLP_PARTS - 1, True)
            norm(N_OUT)

        @block.tensor
        def _(pe):
            def unit(v, src, dv=0, n=S, first=None, rows=None):
                kc = chunks_of(v)
                hi, lo = src
                pe.wait_ge(w_split, v + 1 + 4 * dv)
                if v >= 2 or not isinstance(dv, int):
                    pe.wait_ge(evac[v % 2], v // 2 + 2 * dv)
                wh, wl = whi[v % 2], wlo[v % 2]
                outs = ((bank[v % 2], 0),) if rows is None else rows
                for dst, off in outs:
                    m = P if rows is None else 8
                    for c in range(kc):
                        if first is not None:
                            pe.wait_ge(first[0], first[1] + c + 1)
                        ws = slice(c * P + off, c * P + off + m)
                        nc.tensor.matmul(dst[0:m, 0:n], wh[:, ws], hi[:, c, :], start=c == 0, stop=False)
                        nc.tensor.matmul(dst[0:m, 0:n], wh[:, ws], lo[:, c, :], start=False, stop=False)
                        ins = nc.tensor.matmul(dst[0:m, 0:n], wl[:, ws], hi[:, c, :], start=False, stop=c == kc - 1)
                ins.then_inc(unit_done, 1)

            H, G, M = (hhi, hlo), (ghi, glo), (mem_hi, mem_lo)

            def ada(u, dst, turns=0):
                pe.wait_ge(landed[u % 4], 16 * (u // 4 + 1) + 16 * turns)
                for c in range(DC):
                    ins = nc.tensor.matmul(dst, raw[u % 4][:, c * P:(c + 1) * P], cact[:, c:c + 1], start=c == 0,
                                           stop=c == DC - 1)
                ins.then_inc(ada_done, 1)

            def norm_sum(n):
                w = width(n)
                pe.wait_ge(sq_added, (DC - 1) * (n + 1))
                nc.tensor.matmul(bank[4][:, 0:w], ones, square_sum[:, 0:w], start=True, stop=True).then_inc(sum_done, 1)

            def swiglu(f):
                base, j0 = V_FFN[f], J_FFN[f]
                n = (N_FFN1, N_FFN2)[f]
                for part, kc in enumerate(FF_PARTS):
                    v0, j1, a0 = base + 24 * part, j0 + 8 * part, ADA_PART[part]

                    def body(i, first=None):
                        for k in range(4):
                            unit(v0 + k, H, i, first=first if k == 0 else None)
                            if f == 0:
                                col = (slice(a0 + 4 * i + k, a0 + 4 * i + k + 1) if isinstance(i, int)
                                       else bass.ds(a0 + 4 * i + k, 1))
                                ada(raw_of_ada(a0 + k), bank[7][:, col], 2 * i)

                    body(0, (h_ready, H_AT[n]) if part == 0 else None)
                    with pe.Fori(1, kc // 2) as i:
                        body(i)
                    if f == 0 and part == 2:
                        for a in range(ADA_PART[3], N_ADA):
                            ada(raw_of_ada(a), bank[7][:, a:a + 1])
                    for c in range(DC):
                        unit(v0 + 2 * kc + c, G, first=(op_ready, j1) if c == 0 else None)

            pe.wait_ge(cact_ready, 1)
            for a in range(4):
                ada(a, bank[6][:, a:a + 1])
            with pe.Fori(1, ADA_HEAD_N // 4) as i:
                for k in range(4):
                    ada(k, bank[6][:, bass.ds(4 * i + k, 1)], i)
            for a in range(ADA_HEAD_N, ADA_FIRST):
                ada(a, bank[5][:, a - ADA_HEAD_N:a - ADA_HEAD_N + 1])
            norm_sum(N_FFN1)
            swiglu(0)

            norm_sum(N_MIX)

            def rotate(j):
                v = V_MIX + j
                pe.wait_ge(evac[v % 2], v // 2 + 1)
                if j >= 2:
                    pe.wait_ge(rope_mul, 2 * (j - 1))
                nc.tensor.matmul(bank[2 + j % 2][:], rot, gate_in[j % 2][:], start=True, stop=True).then_inc(rot_done, 1)

            def turn_values(src, dst, nblk):
                for b in range(nblk):
                    ins = nc.tensor.transpose(dst[:, b * P:(b + 1) * P], src[:, b * P:(b + 1) * P], ident)
                ins.then_inc(vT_done, 1)

            for j in range(12):
                unit(V_MIX + j, H, first=(h_ready, H_AT[N_MIX]) if j == 0 else None)
                if 1 <= j <= 10:
                    rotate(j - 1)
                if j == 11:
                    v = V_MIX + 10
                    pe.wait_ge(evac[v % 2], v // 2 + 1)
                    turn_values(gate_in[0], bank[4], NB)

            def scores(i):
                g, n = divmod(i, 4)
                half, lo = (g % 2) * HD, (0 if n else P)
                if i > 0:
                    pe.wait_ge(masked, 2 * i)
                else:
                    pe.wait_ge(rope_done, 10)
                for hh in range(4):
                    ins = nc.tensor.matmul(bank[2 + hh // 2][:, (hh % 2) * 2 * P + lo:(hh % 2 + 1) * 2 * P],
                                           qT[half:half + HD, 4 * (g // 2) + hh, n * P:(n + 1) * P],
                                           kT[half:half + HD, g // 2, (n - 1) * P + lo:(n + 1) * P], start=True, stop=True)
                ins.then_inc(score_done, 1)

            def turn_probs(i, S_, kbs):
                pe.wait_ge(prob_done, i + 1)
                if i > 0:
                    pe.wait_ge(turned_out, i)
                for kb in kbs:
                    for hh in range(4):
                        ins = nc.tensor.transpose(bank[4 + kb][:, hh * P:(hh + 1) * P],
                                                  S_[i % 2][:, hh, kb * P:(kb + 1) * P], ident)
                ins.then_inc(turned, 1)

            def kbs_of(i):
                return range(0 if i % 4 else 1, 2)

            def values(i):
                g, n = divmod(i, 4)
                pe.wait_ge(turned_out, i + 1)
                if i > 0:
                    pe.wait_ge(pv_out, i)
                kbs = kbs_of(i)
                for kb in kbs:
                    ins = nc.tensor.matmul(bank[6][0:HD, :], v_tok[:, n - 1 + kb, g * HD:(g + 1) * HD], probT[:, kb, :],
                                           start=kb == kbs[0], stop=kb == 1)
                ins.then_inc(pv_done, 1)

            v = V_MIX + 11
            pe.wait_ge(evac[v % 2], v // 2 + 1)
            turn_values(gate_in[1], bank[5], NB)
            pe.wait_ge(vtok_done, 2)
            for i in range(16):
                scores(i)
                for a, v in enumerate(slot_units(i)):
                    if v < V_CP:
                        unit(v, H)
                    else:
                        unit(v, H if (v - V_CP) % 2 == 0 else G, first=(op_ready, J_Y) if v == V_CP + 1 else None)
                    if a == 0 and i > 0:
                        values(i - 1)
                turn_probs(i, prob, kbs_of(i))
            values(15)
            for c in range(2 * DC):
                unit(V_AP + c, H if c % 2 == 0 else G, first=(op_ready, J_O) if c == 1 else None)
            for c in range(DC):
                unit(V_WO + c, H, first=(op_ready, J_M) if c == 0 else None)
            norm_sum(N_FFN2)
            swiglu(1)

            norm_sum(N_FINAL)
            norm_sum(N_MIX2)
            unit(V_GATE, H, first=(h_ready, H_AT[N_MIX2]), rows=((bank[V_GATE % 2], 0), (bank[2], 8)))

            def group_unit(v, last=False):
                unit(v, H)
                if v < V_ML:
                    h, k = divmod(v - V_HG, 5)
                    if k == 3:
                        pe.wait_ge(evac[v % 2], v // 2 + 1)
                        if h > 0:
                            pe.wait_ge(vtok_done, 2 + h)
                        turn_values(gate_in[0], bank[5], NB)
                else:
                    h, k = divmod(v - V_ML, 4)
                    if k == 2:
                        pe.wait_ge(evac[v % 2], v // 2 + 1)
                        turn_values(gate_in[0], bank[4], NB)

            for k in range(5):
                group_unit(V_HG + k)
                if k == 4:
                    pe.wait_ge(gate_chain, 13)
                    for dr in range(2):
                        for b in range(NB):
                            at_ = (dr * NB + b) * 8
                            ins = nc.tensor.matmul(bank[3][:, at_:at_ + 8],
                                                   row["a" if dr == 0 else "z"][0:8, b * P:(b + 1) * P],
                                                   ident[0:8, 0:8], start=True, stop=True)
                    ins.then_inc(acol_done, 1)
                    pe.wait_ge(acol_done, 2)

            def hg_items(h, zs):
                s = hg[h % 2]
                for z in zs:
                    if ITEMS * h + z >= 2:
                        pe.wait_ge(lev_taken, ITEMS * h + z - 1)
                    b = bank[2 + z % 2]
                    if z == 0:
                        pe.wait_ge(decay, EVENTS * h + 1)
                        todo = [(blk, normed[1][:, blk * P:(blk + 1) * P], s["q"][:, blk * P:(blk + 1) * P])
                                for blk in range(NB)]
                        w = P
                    elif z <= 2 * LEVELS:
                        m, dr = divmod(z - 1, 2)
                        pe.wait_ge(decay, EVENTS * h + (2 + dr if m == 0 else 4 + dr + 2 * (m - 1)))
                        qq, kk = (q_fwd, s["q"])[dr], s[f"k{dr}"]
                        todo = [(blk, kk[:, blk * P:(blk + 1) * P], qq[:, blk * P:(blk + 1) * P]) for blk in range(NB)]
                        w = P
                    elif z == 2 * LEVELS + 1:
                        pe.wait_ge(decay, EVENTS * h + 5 + 2 * (LEVELS - 1))
                        todo = [(k, s[f"k{k // 2}"][:, a * P:(a + 1) * P], (q_fwd, s["q"])[k // 2][:, t * P:(t + 1) * P])
                                for k, (a, t) in enumerate(((0, 1), (2, 3), (1, 0), (3, 2)))]
                        w = P
                    else:
                        dr = z - 2 * LEVELS - 2
                        pe.wait_ge(decay, EVENTS * h + 4 + dr + 2 * LEVELS)
                        t0 = (S // 2, 0)[dr]
                        qq = (q_fwd, s["q"])[dr][:, t0:t0 + S // 2]
                        todo = [(k, s[f"k{dr}"][:, ((0, 2)[dr] + k) * P:((0, 2)[dr] + k + 1) * P], qq) for k in range(2)]
                        w = S // 2
                    for k, lhs, rhs in todo:
                        ins = nc.tensor.matmul(b[:, k * w:(k + 1) * w], lhs, rhs, start=True, stop=True)
                    ins.then_inc(lev_done, 1)

            def head_sum(h):
                pe.wait_ge(hsq_done, h + 1)
                if NH2 - 1 <= h < 2 * NH2 - 1:
                    pe.wait_ge(vtok_done, 2 + h + 2)
                nc.tensor.matmul(bank[4][:], ones, square[0][:], start=True, stop=True).then_inc(hsum_done, 1)

            for kind, h, units in unit_groups():
                units = list(units)
                if kind == "hg":
                    s = hg[h % 2]
                    for sl in range(5):
                        if units:
                            group_unit(units.pop(0))
                        hg_items(h, ITEM_SLOTS[sl])
                    pe.wait_ge(lev_taken, ITEMS * (h + 1))
                    if h > 0:
                        pe.wait_ge(hnorm_t, h)
                    for b in range(NB):
                        ins = nc.tensor.matmul(bank[6][:], s["v"][:, b * P:(b + 1) * P], scT[:, b * S:(b + 1) * S],
                                               start=b == 0, stop=b == NB - 1)
                    ins.then_inc(o2_done, 1)
                    head_sum(h)
                    continue
                s = ml[h % 2]
                for k in range(4):
                    r0 = (0, 32, 64, 96)[k]
                    if k > 0:
                        pe.wait_ge(bc_out, 4 * h + k)
                    elif h == 0:
                        pe.wait_ge(hnorm_t, NH2)
                    else:
                        pe.wait_ge(abs_done, 2 * h)
                    hd = h + 4 * (k % 2)
                    nc.tensor.matmul(bank[5][:], sel[r0:r0 + 8, hd, :], gate_rows[r0:r0 + 8, :], start=True,
                                     stop=True).then_inc(bc_done, 1)
                pe.wait_ge(qk_done, 2 * h + 2)
                for b in range(NB):
                    if b >= 2:
                        pe.wait_ge(s_mul, 8 * h + 2 * (b - 1))
                    elif h > 0:
                        pe.wait_ge(abs_done, 2 * h)
                    nc.tensor.matmul(bank[2 + b % 2][:], ml_k[:, b * P:(b + 1) * P], ml_q[:], start=True,
                                     stop=True).then_inc(pair_done, 1)
                    if units:
                        group_unit(units.pop(0))
                pe.wait_ge(s_done, 8 * h + 8)
                pe.wait_ge(bc_out, 4 * h + 4)
                if h > 0:
                    pe.wait_ge(ml_step, ML_STEPS * h)
                for dr in range(2):
                    order = range(NB) if dr == 0 else range(NB - 1, -1, -1)
                    for which in range(2):
                        dst = bank[(6, 7)[dr]] if which == 0 else bank[(5, 3)[dr]]
                        for k, b in enumerate(order):
                            t0, t1, at_ = s_range(dr, b)
                            lhs = s["v"][:, b * P:(b + 1) * P] if which == 0 else ones
                            ins = nc.tensor.matmul(dst[:, t0:t1], lhs, sT[dr][:, at_:at_ + t1 - t0], start=k == 0,
                                                   stop=k == NB - 1)
                    ins.then_inc(nd_done, 1)
                head_sum(NH2 + h)

            def x_turn(c):
                v = V_XV + c
                pe.wait_ge(evac[v % 2], v // 2 + 1)
                if c >= 2:
                    pe.wait_ge(vtok_done, 10 + c - 1)
                turn_values(x_vT[c % 2], bank[6 + c % 2], 2)

            for c in range(DC):
                unit(V_WO2 + c, G, first=(op_ready, J_Y2) if c == 0 else None)
            norm_sum(N_MEM)
            for c in range(2 * DC):
                unit(V_XK + c, M, n=MEM, first=(h_ready, H_AT[N_MEM]) if c == 0 else None)
                if c > DC:
                    x_turn(c - DC - 1)
            x_turn(DC - 1)
            norm_sum(N_XATTN)
            for c in range(DC):
                unit(V_XQ + c, H, first=(h_ready, H_AT[N_XATTN]) if c == 0 else None)
            v = V_XQ + DC - 1
            pe.wait_ge(evac[v % 2], v // 2 + 1)
            pe.wait_ge(evac[(v - 1) % 2], (v - 1) // 2 + 1)
            for n in range(NB):
                i = 16 + n
                pe.wait_ge(masked, 2 * i)
                for hh in range(NH2):
                    for e in range(2):
                        ins = nc.tensor.matmul(bank[2 + hh // 2][:, (hh % 2) * 2 * P:(hh % 2 + 1) * 2 * P],
                                               xq[:, 2 * hh + e, n * P:(n + 1) * P], xk[:, 2 * hh + e, :], start=e == 0,
                                               stop=e == 1)
                ins.then_inc(score_done, 1)
                turn_probs(i, x_prob, range(2))
                pe.wait_ge(turned_out, i + 1)
                pe.wait_ge(pv_out, i)
                for hh in range(NH2):
                    for e in range(2):
                        at_ = ((hh % 2) * 2 + e) * P
                        for kb in range(2):
                            ins = nc.tensor.matmul(bank[6 + hh // 2][:, at_:at_ + P],
                                                   xv[:, kb, (2 * hh + e) * P:(2 * hh + e + 1) * P],
                                                   x_probT[:, kb, hh * P:(hh + 1) * P], start=kb == 0, stop=kb == 1)
                ins.then_inc(pv_done, 1)
            for c in range(DC):
                unit(V_XO + c, G, first=(op_ready, J_XO) if c == 0 else None)
            norm_sum(N_MLP)

            def mlp(i, first):
                for c in range(DC):
                    unit(V_MLP + c, H, 4 * i, first=first if c == 0 else None)
                for c in range(DC):
                    unit(V_MLP + DC + c, G, 4 * i, first=(op_ready, J_MLP + DC * i) if c == 0 else None)

            mlp(0, (h_ready, H_AT[N_MLP]))
            with pe.Fori(1, MLP_PARTS) as i:
                mlp(i, None)
            norm_sum(N_OUT)


def constants():
    con = np.zeros((P, N_CON), np.float32)
    i = np.arange(P)
    con[i, CON["ident"] + i] = 1
    con[:, CON["ones"]:CON["ones"] + P] = 1
    for half in (0, HD):
        k = half + np.arange(HD // 2)
        con[k + HD // 2, CON["rot"] + k] = -1
        con[k, CON["rot"] + k + HD // 2] = 1
    con[:, CON["tri"]:CON["tri"] + P] = i[:, None] <= i[None, :]
    con[:, CON["tri"] + P:CON["tri"] + 2 * P] = i[:, None] >= i[None, :]
    diff = P + i[:, None] - np.arange(2 * P)[None, :]
    con[:, CON["win"]:CON["win"] + 2 * P] = np.where((diff >= 0) & (diff < P), 0, -1e30)
    for base in (0, 32, 64, 96):
        for r in range(8):
            con[base + r, CON["sel"] + r * P:CON["sel"] + (r + 1) * P] = 1
    mask = np.zeros((P, 2 * LEVELS, P), np.float32)
    for m in range(LEVELS):
        same = (i[:, None] >> (m + 1)) == (i[None, :] >> (m + 1))
        late = (i >> m) & 1
        mask[:, 2 * m] = same & (late[:, None] == 0) & (late[None, :] == 1)
        mask[:, 2 * m + 1] = same & (late[:, None] == 1) & (late[None, :] == 0)
    inv = 1.0 / (np.float32(10000.0) ** (np.arange(0, HD, 2, dtype=np.float32) / HD))
    ang = (np.arange(S, dtype=np.float32)[:, None] * inv.astype(np.float32)[None, :]).T
    rope = np.stack([np.tile(np.cos(ang), (4, 1)), np.tile(np.sin(ang), (4, 1))], axis=1)
    return con, np.ascontiguousarray(rope, dtype=np.float32), mask


def tiles(w):
    k, n = w.shape
    return w.reshape(k // P, P, n // P, P).transpose(2, 1, 0, 3).reshape(n // P, P, k)


def feature_major(x):
    t, d = x.shape
    return np.ascontiguousarray(x.reshape(t, d // P, P).transpose(2, 1, 0))


def in_turn(*units):
    return np.stack(units, axis=1).reshape(-1, *units[0].shape[1:])


def pack(a):
    heads = np.array([[4 * (2 * m + half) + j for half in range(2)] for m in range(2) for j in range(4)]).ravel()
    order = (heads[:, None] * HD + np.arange(HD)).ravel()

    def swiglu(w_gu, w_down):
        gu = in_turn(tiles(w_gu[:, :FF]), tiles(w_gu[:, FF:]))
        out, at = [], 0
        for kc in FF_PARTS:
            out.append((gu[2 * at:2 * (at + kc)], tiles(w_down[at * P:(at + kc) * P])))
            at += kc
        return out

    ada = tiles(a["w_ada"][0])
    w8, w6 = [ada[:ADA_FIRST]], []
    for part, (gu, down) in enumerate(swiglu(a["w1_gu"][0], a["w1_down"][0])):
        w8.append(in_turn(gu, ada[ADA_PART[part]:ADA_PART[part] + len(gu)]))
        if part == 2:
            w8.append(ada[ADA_PART[3]:])
        (w8 if down.shape[2] == D else w6).append(down)
    w_in = a["w_in"][0]
    b, c, u, q, k, v, zc, za = np.split(w_in, np.cumsum([D, D, D, D, 256, 256, D]), axis=1)
    w8 += [tiles(q[:, order]), tiles(k), tiles(v), in_turn(tiles(c), tiles(u), tiles(b)),
           in_turn(tiles(zc), tiles(a["w_conv_proj"][0])), in_turn(tiles(za), tiles(a["w_attn_proj"][0][order])),
           tiles(a["w_out"][0])]
    for gu, down in swiglu(a["w2_gu"][0], a["w2_down"][0]):
        w8.append(gu)
        (w8 if down.shape[2] == D else w6).append(down)
    w_in = a["w_in_2"][0]
    gates = np.zeros((D, P), np.float32)
    gates[:, :16] = w_in[:, 36 * P:]
    t = tiles(w_in[:, :36 * P]).reshape(9, 4, P, D)
    w8 += [tiles(gates), t[:5].transpose(1, 0, 2, 3).reshape(-1, P, D), t[5:].transpose(1, 0, 2, 3).reshape(-1, P, D),
           tiles(a["w_out_2"][0]), tiles(a["w_xkv_2"][0]), tiles(a["w_xq_2"][0]), tiles(a["w_xo_2"][0])]
    up = tiles(a["w_up_2"][0])
    for part in range(MLP_PARTS):
        w8 += [up[part * DC:(part + 1) * DC], tiles(a["w_down_2"][0][part * D:(part + 1) * D])]
    return np.concatenate(w8), np.concatenate(w6)


def pack_vectors(a):
    def cols(x):
        return x.reshape(-1, P).T

    vec = np.zeros((P, N_VEC), np.float32)
    gains = [a[n].reshape(-1) for n in ("g_ffn1", "g_mix", "g_ffn2", "g_final", "norm_mix_2", "norm_mem_2",
                                        "norm_xattn_2", "norm_mlp_2", "norm_final_2")]
    b_in = a["b_in_2"][0]
    for name, x in (("c", cols(a["c"])), ("b_ada", cols(a["b_ada"])), ("gain", cols(np.concatenate(gains))),
                    ("conv_w", cols(a["conv_w"])), ("b_in", cols(b_in[:36 * P])),
                    ("b_gate", b_in[36 * P:].reshape(2, 8).T), ("lb", cols(a["hgrn_lb_logits_2"])),
                    ("hgrn_g", cols(a["hgrn_norm_2"])), ("mconv_w", cols(a["mlstm_conv_w_2"])),
                    ("mconv_b", cols(a["mlstm_conv_b_2"])), ("mlstm_g", cols(a["mlstm_norm_2"])),
                    ("sinks", np.broadcast_to(a["sinks"].reshape(1, N_Q), (P, N_Q)))):
        vec[:x.shape[0], VEC[name]:VEC[name] + x.shape[1]] = x
    return vec


def kernel(**inputs):
    import concourse.bacc as bacc
    from concourse.bass_utils import run_bass_kernel_spmd

    a = {k: np.asarray(v) for k, v in inputs.items()}
    con, rope, mask = constants()
    w8, w6 = pack(a)
    arrays = {"x_t": feature_major(a["x"][0]), "mem_t": feature_major(a["mem_2"][0]), "vectors": pack_vectors(a),
              "constants": con, "rope": rope, "level_mask_in": mask, "w8": w8, "w6": w6}
    nc = bacc.Bacc("TRN2", target_bir_lowering=False, num_devices=1)
    args = [nc.dram_tensor(n, x.shape, mybir.dt.from_np(x.dtype), kind="ExternalInput").ap() for n, x in arrays.items()]
    args.append(nc.dram_tensor("y_t", (P, DC, S), F32, kind="ExternalOutput").ap())
    build(nc, *args)
    y = run_bass_kernel_spmd(nc, [arrays], core_ids=[0]).results[0]["y_t"]
    return np.ascontiguousarray(y.transpose(2, 1, 0)).reshape(1, S, D)
```

```python
from contextlib import ExitStack

import numpy as np
import concourse.bass as bass
from concourse import mybir

ALU = mybir.AluOpType
ACT = mybir.ActivationFunctionType
AX_X = mybir.AxisListType.X
F32 = mybir.dt.float32
F32R = mybir.dt.float32r
U8 = mybir.dt.uint8

P = 128
S = 512
D = 1024
DC = D // P
NB = S // P
EPS = 1e-6
N_MOD = 9
N_ADA = N_MOD * DC
FF = 2816
FF_PARTS = (8, 8, 6)
HD = 64
N_KV = 4
N_Q = 16
MEM = 256
NH2 = 4
LEVELS = 7
ITEMS = 2 * LEVELS + 4
EVENTS = 3 + 2 * (LEVELS + 1)
ML_STEPS = 7
MLP_PARTS = 4
SCORE_SCALE = HD ** -0.5
XATTN_SCALE = (D // NH2) ** -0.5
MLSTM_SCALE = P ** -0.5

V_FFN_LEN = 2 * (FF // P) + len(FF_PARTS) * DC
V_MIX = V_FFN_LEN
V_CONV = V_MIX + 12
V_CP = V_CONV + 24
V_AP = V_CP + 16
V_WO = V_AP + 16
V_FFN = (0, V_WO + DC)
V_GATE = V_FFN[1] + V_FFN_LEN
V_HG = V_GATE + 1
V_ML = V_HG + 5 * NH2
V_WO2 = V_ML + 4 * NH2
V_XK = V_WO2 + DC
V_XV = V_XK + DC
V_XQ = V_XV + DC
V_XO = V_XQ + DC
V_MLP = V_XO + DC
V_END = V_MLP + 2 * MLP_PARTS * DC
ADA_HEAD_N = 2 * DC
ADA_TAIL = 4
ADA_PART = (16, 36, 56, 72)
PART_LEN = 44


def raw_of(v):
    if v >= V_FFN_LEN:
        return v + N_ADA
    part = v // 24
    base, k, gu = ADA_HEAD_N + PART_LEN * part, v - 24 * part, 2 * FF_PARTS[part]
    return base + 2 * k if k < gu + ADA_TAIL else base + gu + ADA_TAIL + k


def raw_of_ada(a):
    if a < ADA_HEAD_N:
        return a
    part = sum(a >= start for start in ADA_PART[1:])
    return ADA_HEAD_N + PART_LEN * part + 2 * (a - ADA_PART[part]) + 1


def chunks_of(v):
    return FF_PARTS[2] if any(base + 60 <= v < base + V_FFN_LEN for base in V_FFN) else DC


J_FFN = (0, 46)
J_Y, J_O, J_M = 22, 30, 38
J_Y2, J_XO, J_MLP = 68, 76, 84

N_FFN1, N_MIX, N_FFN2, N_FINAL, N_MIX2, N_MEM, N_XATTN, N_MLP, N_OUT = range(9)


def columns(*names):
    at, where = 0, {}
    for name, n in names:
        where[name] = at
        at += n
    return where, at


VEC, N_VEC = columns(("c", DC), ("b_ada", N_ADA), ("gain", 9 * DC), ("conv_w", 3 * DC), ("b_in", 36), ("b_gate", 2),
                     ("lb", 8), ("hgrn_g", NH2), ("mconv_w", 5 * DC), ("mconv_b", DC), ("mlstm_g", NH2),
                     ("sinks", N_Q))
CON, N_CON = columns(("ident", P), ("ones", P), ("rot", P), ("tri", 2 * P), ("win", 2 * P), ("sel", 8 * P))
SUM, NEG_MAX, SINK, DEN, RDEN, ROW_MAX = range(6)


def build(nc, x_in, mem_in, vec_in, con_in, rope_in, mask_in, w8_in, w6_in, out):
    with ExitStack() as ctx:
        def sb(name, shape, dt=F32):
            return ctx.enter_context(nc.sbuf_tensor(name, shape, dt))

        def sem(name):
            return ctx.enter_context(nc.semaphore(name))

        bank = [ctx.enter_context(nc.psum_tensor(f"bank{i}", [P, S], F32)) for i in range(8)]

        raw = [sb(f"raw{i}", [P, DC * P]) for i in range(4)]
        whi = [sb(f"whi{i}", [P, DC * P], F32R) for i in range(2)]
        wlo = [sb(f"wlo{i}", [P, DC * P], F32R) for i in range(2)]
        xT = sb("xT", [P, DC, S])
        hhi = sb("hhi", [P, DC, S], F32R)
        hlo = sb("hlo", [P, DC, S], F32R)
        ghi = sb("ghi", [P, DC, S], F32R)
        glo = sb("glo", [P, DC, S], F32R)
        mem_hi = hhi[:, 4:8, :].rearrange("p c (a t) -> p (c a) t", t=MEM)
        mem_lo = hlo[:, 4:8, :].rearrange("p c (a t) -> p (c a) t", t=MEM)

        vec = sb("vec", [P, N_VEC])
        con = sb("con", [P, N_CON])
        level_mask = sb("level_mask", [P, 2 * LEVELS, P], U8)
        mods = sb("mods", [P, N_ADA])
        gscale = sb("gscale", [P, 9 * DC])
        cact = sb("cact", [P, DC])
        zero_col = sb("zero_col", [P, 1])
        eps_col = sb("eps_col", [P, 1])
        neg_b_in = sb("neg_b_in", [P, 36])
        lbs = sb("lbs", [P, 2, 8])
        lbt = sb("lbt", [P, 3, 8])
        neg_sink = sb("neg_sink", [P, N_Q])
        stat = sb("stat", [P, 2, 6, 4])
        acol = sb("acol", [P, 2, NB, 8])

        square = [sb(f"square{i}", [P, S]) for i in range(2)]
        square_sum = sb("square_sum", [P, S])
        rstd = sb("rstd", [P, S])
        normed = [sb(f"normed{i}", [P, S]) for i in range(2)]
        gate_in = [sb(f"gate_in{i}", [P, S]) for i in range(2)]
        opnd = [sb(f"opnd{i}", [P, S]) for i in range(2)]

        WORK = 16100
        work = sb("work", [P, WORK])
        at = [0]

        def place(*shape):
            n = int(np.prod(shape))
            assert at[0] + n <= WORK, (at, n)
            a = work[:, at[0]:at[0] + n]
            at[0] += n
            return a.rearrange("p (a b) -> p a b", b=shape[1]) if len(shape) == 2 else a

        qT = place(DC, S)
        kT = place(2, S)
        v_tok = place(NB, N_KV * HD)
        rope = place(2, S)
        conv_in = [place(S + 2) for _ in range(2)]
        conv_out = place(S)
        merged = place(DC, S)
        ada_acc = [merged[:, 0, i * P:(i + 1) * P] for i in range(4)]
        prob = [place(4, 2 * P) for _ in range(2)]
        probT = place(2, S)
        rope_a, rope_b = prob[0], prob[1]
        mask_f32 = qT[:, 0:4, :].rearrange("p a b -> p (a b)")[:, 0:2 * LEVELS * P]
        mask_f32 = mask_f32.rearrange("p (a b) -> p a b", b=P)
        at[0] = 0
        hg = [{n: place(S) for n in ("q", "f0", "k0", "f1", "k1", "g", "v")} for _ in range(2)]
        q_fwd = place(S)
        fprod = [place(S) for _ in range(2)]
        scT = place(NB * (S + P))
        ml = [{"q": place(S + 4), "k": place(S + 4), "v": place(S), "o": place(S)} for _ in range(2)]
        gate_rows = place(S)
        assert at[0] <= WORK
        at[0] = 0
        ml_q, ml_k = place(S), place(S)
        neg_m = [place(S) for _ in range(2)]
        em = [place(S) for _ in range(2)]
        dmat = [place(S) for _ in range(2)]
        sT = [place(NB * (NB + 1) // 2 * P) for _ in range(2)]
        ml_h = [place(S) for _ in range(2)]
        assert at[0] <= 14 * S + 4 * S + NB * (S + P)
        at[0] = 7 * S
        row = {n: place(S) for n in ("ig", "z", "t", "lf", "cum0", "cum1", "a")}
        at[0] = 0
        memT = place(DC, MEM)
        xk = place(DC, MEM)
        xv = place(2, D)
        xq = place(DC, S)
        x_prob = [place(4, 2 * P) for _ in range(2)]
        x_probT = place(2, S)
        x_vT = [place(MEM) for _ in range(2)]

        ident = con[:, CON["ident"]:CON["ident"] + P]
        ones = con[:, CON["ones"]:CON["ones"] + P]
        rot = con[:, CON["rot"]:CON["rot"] + P]
        tri = con[:, CON["tri"]:CON["tri"] + 2 * P].rearrange("p (a b) -> p a b", b=P)
        win = con[:, CON["win"]:CON["win"] + 2 * P]
        sel = con[:, CON["sel"]:CON["sel"] + 8 * P].rearrange("p (a b) -> p a b", b=P)

        def vcol(name, i=0, rows=P):
            return vec[0:rows, VEC[name] + i:VEC[name] + i + 1]

        def mod(kind, c):
            return mods[:, kind * DC + c:kind * DC + c + 1]

        SH = {N_FFN1: 0, N_MIX: 3, N_FFN2: 6}

        def shift(n, c):
            return mod(SH[n], c) if n in SH else zero_col[:, 0:1]

        small_in, con_landed, mask_landed = sem("small_in"), sem("con_landed"), sem("mask_landed")
        rope_in_s = sem("rope_landed")
        x_landed = sem("x_landed")
        mem_landed = sem("mem_landed")
        landed = [sem(f"landed{i}") for i in range(4)]
        w_hi = sem("w_hi")
        w_split = sem("w_split")
        unit_done = sem("unit_done")
        evac = [sem(f"evac{i}") for i in range(2)]
        ada_step = sem("ada_step")
        ada_done = sem("ada_done")
        cact_ready = sem("cact_ready")
        setup_v = sem("setup_v")
        setup_a = sem("setup_a")
        mods_done = sem("mods_done")
        sq_done, sq_added, sum_done = sem("sq_done"), sem("sq_added"), sem("sum_done")
        rstd_ln, rstd_done = sem("rstd_ln"), sem("rstd_done")
        normed_done, h_hi, h_ready = sem("normed_done"), sem("h_hi"), sem("h_ready")
        op_src, op_hi, op_ready = sem("op_src"), sem("op_hi"), sem("op_ready")
        rot_done, rope_mul, rope_done = sem("rot_done"), sem("rope_mul"), sem("rope_done")
        vT_done, vtok_done = sem("vT_done"), sem("vtok_done")
        conv_step, pad_done = sem("conv_step"), sem("pad_done")
        score_done, masked, row_max, neg_max = sem("score_done"), sem("masked"), sem("row_max"), sem("neg_max")
        sink_sum, exp_done, den_done, rden_done = sem("sink_sum"), sem("exp_done"), sem("den_done"), sem("rden_done")
        prob_done, turned, turned_out = sem("prob_done"), sem("turned"), sem("turned_out")
        pv_done, pv_out, x_half = sem("pv_done"), sem("pv_out"), sem("x_half")
        gated = sem("gated")
        gate_chain, acol_done = sem("gate_chain"), sem("acol_done")
        sig_done, fk_done = sem("sig_done"), sem("fk_done")
        lev_done, lev_taken, decay = sem("lev_done"), sem("lev_taken"), sem("decay")
        o2_done, hsq_done, hsum_done, hln_done, hrs_done, hnorm_t = (
            sem("o2_done"), sem("hsq_done"), sem("hsum_done"), sem("hln_done"), sem("hrs_done"), sem("hnorm_t"))
        tap_done, qk_done, bc_done, bc_out = sem("tap_done"), sem("qk_done"), sem("bc_done"), sem("bc_out")
        pair_done, d_arg, d_exp, s_mul, s_done = sem("pair_done"), sem("d_arg"), sem("d_exp"), sem("s_mul"), sem("s_done")
        nd_done, abs_done, ml_step = sem("nd_done"), sem("abs_done"), sem("ml_step")
        relu_done = sem("relu_done")
        out_v, stored = sem("out_v"), sem("stored")

        block = ctx.enter_context(nc.Block())

        def x_ready(eng, n, c):
            if n == N_FFN1:
                return eng.wait_ge(x_landed, 16)
            if n == N_MEM:
                return eng.wait_ge(mem_landed, 16)
            if n == N_MIX2:
                return eng.wait_ge(normed_done, DC * N_FINAL + c + 1)
            v = {N_MIX: V_MIX - DC, N_FFN2: V_WO, N_FINAL: V_GATE - DC, N_XATTN: V_WO2, N_MLP: V_XO,
                 N_OUT: V_END - DC}[n] + c
            eng.wait_ge(evac[v % 2], v // 2 + 1)

        def norm_src(n, c):
            return memT[:, c, :] if n == N_MEM else xT[:, c, :]

        def width(n):
            return MEM if n == N_MEM else S

        H_AT = {N_FFN1: 0, N_MIX: 8, N_FFN2: 16, N_MIX2: 24, N_MEM: 32, N_XATTN: 40, N_MLP: 48}

        def h_out(n, c):
            return (mem_hi[:, c, :], mem_lo[:, c, :]) if n == N_MEM else (hhi[:, c, :], hlo[:, c, :])

        def pairs(t, m):
            return t.rearrange("p (j a m) -> p j a m", a=2, m=m)

        def fsrc(s, dr, k):
            if k == 0:
                return s[f"f{dr}"]
            n = S >> k
            return fprod[dr][:, S - 2 * n:S - n]

        diag = scT[:, :].rearrange("p (b c) -> p b c", c=S + P)[:, :, 0:P]

        def slot_units(i):
            return range(V_CONV + 2 * i, V_CONV + 2 * i + 2) if i < 12 else range(V_CP + 4 * (i - 12), V_CP + 4 * (i - 11))

        def s_range(dr, b):
            if dr == 0:
                return b * P, S, sum(S - i * P for i in range(b))
            return 0, (b + 1) * P, sum((i + 1) * P for i in range(b))

        def unit_groups():
            out = []
            for h in range(NH2):
                nxt = range(V_HG + 5 * (h + 1), V_HG + 5 * (h + 2)) if h + 1 < NH2 else range(V_ML, V_ML + 4)
                out.append(("hg", h, list(nxt)))
            for h in range(NH2):
                out.append(("ml", h, list(range(V_ML + 4 * (h + 1), V_ML + 4 * (h + 2))) if h + 1 < NH2 else []))
            return out

        ITEM_SLOTS = [range(0, 4), range(4, 7), range(7, 10), range(10, 14), range(14, ITEMS)]

        @block.sync
        def _(sp):
            sp.dma_start(vec[:], vec_in).then_inc(small_in, 16)

            def load(u, w, kc=DC):
                src = w8_in if kc == DC else w6_in
                sp.dma_start(raw[u % 4][:, 0:kc * P], src[w]).then_inc(landed[u % 4], 16)

            user = {raw_of(v): (w_split, v + 1) for v in range(V_END)}
            user |= {raw_of_ada(a): (ada_step, DC * (a + 1)) for a in range(N_ADA)}

            def load_at(u, w, kc=DC):
                if u >= 4:
                    sp.wait_ge(*user[u - 4])
                load(u, w, kc)

            for u in range(4):
                load_at(u, u)
            with sp.Fori(1, ADA_HEAD_N // 4) as i:
                for k in range(4):
                    sp.wait_ge(ada_step, DC * (k - 3) + 4 * DC * i)
                    load(k, 4 * i + k)
            for part, kc in enumerate(FF_PARTS):
                v0, a0 = 24 * part, ADA_PART[part]
                u0 = raw_of(v0)
                for u in range(u0, u0 + 8):
                    load_at(u, u)
                with sp.Fori(1, kc // 2) as i:
                    for k in range(4):
                        sp.wait_ge(w_split, v0 + k - 1 + 4 * i)
                        load(u0 + 2 * k, u0 + 2 * k + 8 * i)
                        sp.wait_ge(ada_step, DC * (a0 + k - 1) + 4 * DC * i)
                        load(u0 + 2 * k + 1, u0 + 2 * k + 1 + 8 * i)
                for c in range(DC):
                    u = raw_of(v0 + 2 * kc + c)
                    load_at(u, u if kc == DC else c, kc)
                    if c < ADA_TAIL:
                        load_at(u + 1, u + 1 if kc == DC else u0 + 4 * kc + c)

            def run(v0, v1, w0, kc=DC):
                for k in range(4):
                    load_at(raw_of(v0 + k), w0 + k, kc)
                if v1 - v0 >= 8:
                    with sp.Fori(1, (v1 - v0) // 4) as i:
                        for k in range(4):
                            sp.wait_ge(w_split, v0 + k - 3 + 4 * i)
                            load(raw_of(v0 + k), w0 + k + 4 * i, kc)
                for k in range((v1 - v0) // 4 * 4, v1 - v0):
                    load_at(raw_of(v0 + k), w0 + k, kc)

            down2 = V_FFN[1] + 60
            row0 = raw_of(V_MIX) - DC
            run(V_MIX, down2, row0)
            run(down2, V_GATE, DC, FF_PARTS[2])
            run(V_GATE, V_END, row0 + down2 - V_MIX)
            sp.wait_ge(stored, 16 * DC)

        @block.gpsimd
        def _(pool):
            pool.dma_start(xT[:], x_in).then_inc(x_landed, 16)
            pool.dma_start(con[:], con_in).then_inc(con_landed, 16)
            pool.dma_start(rope, rope_in).then_inc(rope_in_s, 16)
            pool.dma_start(mask_f32, mask_in).then_inc(mask_landed, 16)
            for n in range(9):
                w = width(n)
                if n == N_MEM:
                    pool.wait_ge(op_ready, J_Y2 + DC)
                    pool.dma_start(memT, mem_in).then_inc(mem_landed, 16)
                for c in range(1, DC - 1):
                    pool.wait_ge(sq_done, DC * n + c + 1)
                    if c > 1:
                        pool.wait_ge(sq_added, (DC - 2) * n + c - 1)
                    nc.gpsimd.tensor_tensor(square_sum[:, 0:w], square_sum[:, 0:w], square[c % 2][:, 0:w],
                                            ALU.add).then_inc(sq_added, 1)

        @block.scalar
        def _(act):
            nxt = [0]

            def split(v, dv=0, u=None, du=0):
                kc = chunks_of(v)
                u = raw_of(v) if u is None else u
                act.wait_ge(landed[u % 4], 16 * (u // 4 + 1) + 16 * du)
                if v >= 2 or not isinstance(dv, int):
                    act.wait_ge(unit_done, v - 1 + 4 * dv)
                nc.scalar.activation(whi[v % 2][:, 0:kc * P], raw[u % 4][:, 0:kc * P], ACT.Copy).then_inc(w_hi, 1)

            def split_next(v):
                if nxt[0] <= v + 1 < V_END:
                    split(v + 1)
                    nxt[0] = v + 2

            def norm_square(n, c):
                w = width(n)
                x_ready(act, n, c)
                if c == 0 and n > 0:
                    act.wait_ge(sum_done, n)
                if c > 2:
                    act.wait_ge(sq_added, (DC - 2) * n + c - 2)
                dst = square_sum if c == 0 else square[c % 2]
                nc.scalar.activation(dst[:, 0:w], norm_src(n, c), ACT.Square).then_inc(sq_done, 1)

            def norm_stats(n, start=0):
                w = width(n)
                for c in range(start, DC):
                    norm_square(n, c)
                act.wait_ge(sum_done, n + 1)
                if n > 0:
                    act.wait_ge(normed_done, DC * n)
                nc.scalar.activation(rstd[:, 0:w], bank[4][:, 0:w], ACT.Ln, bias=eps_col[:, 0:1],
                                     scale=1.0 / D).then_inc(rstd_ln, 1)
                act.wait_ge(rstd_ln, n + 1)
                nc.scalar.activation(rstd[:, 0:w], rstd[:, 0:w], ACT.Exp, scale=-0.5).then_inc(rstd_done, 1)

            def norm_hi(n, free=None):
                w = width(n)
                for c in range(DC):
                    act.wait_ge(normed_done, DC * n + c + 1)
                    if free is not None and c == 0:
                        act.wait_ge(unit_done, free)
                    nc.scalar.activation(h_out(n, c)[0], normed[c % 2][:, 0:w], ACT.Identity,
                                         bias=shift(n, c)).then_inc(h_hi, 1)

            def operand_hi(j, c):
                nc.scalar.activation(ghi[:, c, :], opnd[j % 2][:], ACT.Copy).then_inc(op_hi, 1)

            def evacuate(v, out_ap, func, bias=None, scale=1.0, n=S):
                b = bank[v % 2][:, 0:n]
                if bias is None:
                    nc.scalar.activation(out_ap, b, func, scale=scale).then_inc(evac[v % 2], 1)
                else:
                    nc.scalar.activation(out_ap, b, func, bias=bias, scale=scale).then_inc(evac[v % 2], 1)

            def swiglu(f):
                base, j0 = V_FFN[f], J_FFN[f]
                for part, kc in enumerate(FF_PARTS):
                    v0, j1 = base + 24 * part, j0 + 8 * part

                    def body(i, last):
                        ru = 2 if f == 0 else 1
                        for k in range(2):
                            v = v0 + 2 * k
                            split(v + 1, i, raw_of(v + 1), ru * i)
                            act.wait_ge(unit_done, v + 1 + 4 * i)
                            nc.scalar.activation(gate_in[k][:], bank[0][:], ACT.Silu).then_inc(evac[0], 1)
                            if k == 0:
                                split(v + 2, i, raw_of(v + 2), ru * i)
                            elif not last:
                                split(v0, i + 1, raw_of(v0), ru * (i + 1))
                            else:
                                split(v + 2 + 4 * i)
                            act.wait_ge(evac[1], (v + 1) // 2 + 1 + 2 * i)
                            if isinstance(i, int):
                                g = slice(2 * i + k, 2 * i + k + 1)
                            else:
                                g = bass.ds(2 * i + k, 1)
                                act.wait_ge(small_in, 16)
                            nc.scalar.activation(ghi[:, g, :], opnd[k][:].unsqueeze(1), ACT.Copy).then_inc(op_hi, 1)

                    body(0, False)
                    with act.Fori(1, kc // 2 - 1) as i:
                        body(i, False)
                    body(kc // 2 - 1, True)
                    for c in range(DC):
                        split(v0 + 2 * kc + c + 1)
                        if part == 2 and c > 0:
                            norm_square((N_MIX, N_FINAL)[f], c - 1)
                nxt[0] = base + V_FFN_LEN + 1

            act.wait_ge(small_in, 16)
            nc.scalar.activation(cact[:], vec[:, VEC["c"]:VEC["c"] + DC], ACT.Silu).then_inc(cact_ready, 1)
            act.wait_ge(setup_v, 1)
            nc.scalar.activation(lbt[:, 1, :], lbt[:, 0, :], ACT.Exp).then_inc(setup_a, 1)
            norm_stats(N_FFN1)
            split(0)
            norm_hi(N_FFN1)
            swiglu(0)

            norm_stats(N_MIX, DC - 1)
            norm_hi(N_MIX)
            for j in range(10):
                v = V_MIX + j
                split_next(v)
                act.wait_ge(unit_done, v + 1)
                if j >= 2:
                    act.wait_ge(rope_mul, 2 * (j - 1))
                evacuate(v, gate_in[j % 2][:], ACT.Copy)
            for t in range(2):
                v = V_MIX + 10 + t
                split_next(v)
                act.wait_ge(unit_done, v + 1)
                act.wait_ge(rope_mul, 2 * (9 + t))
                evacuate(v, gate_in[t][:], ACT.Copy)

            def step_exp(i, S_, n_keys_lo, sink):
                act.wait_ge(neg_max, i + 1)
                for hh in range(4):
                    ins = nc.scalar.activation(S_[i % 2][:, hh, n_keys_lo:], S_[i % 2][:, hh, n_keys_lo:], ACT.Exp,
                                               bias=stat[:, i % 2, NEG_MAX, hh:hh + 1],
                                               accum_out=stat[:, i % 2, SUM, hh:hh + 1])
                if sink:
                    act.wait_ge(sink_sum, i + 1)
                    ins = nc.scalar.activation(stat[:, i % 2, SINK, :], stat[:, i % 2, SINK, :], ACT.Exp)
                ins.then_inc(exp_done, 1)

            def step_turned(i, dst, kbs):
                act.wait_ge(turned, i + 1)
                if i > 0:
                    act.wait_ge(pv_done, i)
                for kb in kbs:
                    ins = nc.scalar.activation(dst[:, kb, :], bank[4 + kb][:], ACT.Copy)
                ins.then_inc(turned_out, 1)

            def kbs_of(i):
                return range(0 if i % 4 else 1, 2)

            def conv_unit(v):
                c, k = divmod(v - V_CONV, 3)
                split_next(v)
                if k == 0:
                    act.wait_ge(unit_done, v + 1)
                    if c == 0:
                        act.wait_ge(vT_done, 2)
                    elif c >= 2:
                        vp = V_CONV + 3 * (c - 2) + 1
                        act.wait_ge(evac[vp % 2], vp // 2 + 1)
                    evacuate(v, gate_in[c % 2][:], ACT.Copy)
                if k == 2:
                    act.wait_ge(evac[v % 2], v // 2 + 1)
                    operand_hi(J_Y + c, c)

            def gate_unit(v, base):
                c, k = divmod(v - base, 2)
                split_next(v)
                if k == 0:
                    act.wait_ge(unit_done, v + 1)
                    if v >= V_CP + 4:
                        act.wait_ge(evac[(v - 3) % 2], (v - 3) // 2 + 1)
                    else:
                        vp = V_CONV + 3 * (6 + c) + 1
                        act.wait_ge(evac[vp % 2], vp // 2 + 1)
                    evacuate(v, gate_in[c % 2][:], ACT.Sigmoid)

            for i in range(16):
                units = slot_units(i)
                lo = 0 if i % 4 else P
                for a, v in enumerate(units):
                    (conv_unit if v < V_CP else lambda u: gate_unit(u, V_CP))(v)
                    if a == 0:
                        step_exp(i, prob, lo, True)
                        if i > 0:
                            step_turned(i - 1, probT, kbs_of(i - 1))
            step_turned(15, probT, kbs_of(15))
            for c in range(DC):
                act.wait_ge(pv_out, 16)
                if c == 0:
                    act.wait_ge(unit_done, V_AP)
                nc.scalar.activation(ghi[:, c, :], qT[:, c, :], ACT.Copy).then_inc(op_hi, 1)
            for c in range(2 * DC):
                gate_unit(V_AP + c, V_AP)
            for c in range(DC):
                act.wait_ge(gated, DC)
                act.wait_ge(unit_done, V_WO)
                nc.scalar.activation(hhi[:, c, :], merged[:, c, :], ACT.Copy).then_inc(op_hi, 1)
            for c in range(DC):
                split_next(V_WO + c)
                if c > 0:
                    norm_square(N_FFN2, c - 1)
            norm_stats(N_FFN2, DC - 1)
            norm_hi(N_FFN2)
            swiglu(1)

            norm_stats(N_FINAL, DC - 1)
            norm_stats(N_MIX2)
            norm_hi(N_MIX2)
            split_next(V_GATE)

            def b_in(i):
                return vcol("b_in", i)

            act.wait_ge(unit_done, V_GATE + 1)
            nc.scalar.activation(row["ig"][0:8, :], bank[V_GATE % 2][0:8, :], ACT.Identity,
                                 bias=vcol("b_gate", 0, 8)).then_inc(evac[V_GATE % 2], 1)
            nc.scalar.activation(row["z"][0:8, :], bank[2][0:8, :], ACT.Identity,
                                 bias=vcol("b_gate", 1, 8)).then_inc(gate_chain, 1)
            act.wait_ge(gate_chain, 1)
            nc.scalar.activation(row["t"][0:8, :], row["z"][0:8, :], ACT.Abs).then_inc(gate_chain, 1)
            act.wait_ge(gate_chain, 2)
            nc.scalar.activation(row["t"][0:8, :], row["t"][0:8, :], ACT.Exp, scale=-1.0).then_inc(gate_chain, 1)
            act.wait_ge(gate_chain, 3)
            nc.scalar.activation(row["t"][0:8, :], row["t"][0:8, :], ACT.Ln, bias=1.0).then_inc(gate_chain, 1)

            def group_unit(v):
                split_next(v)
                if v < V_ML:
                    h, k = divmod(v - V_HG, 5)
                    s = hg[h % 2]
                    col = (0, 4, 8, 12, 16)[k] + h
                    act.wait_ge(unit_done, v + 1)
                    if h >= 2 and k == 0:
                        act.wait_ge(lev_done, ITEMS * (h - 1))
                    if h == 1 and k == 0:
                        act.wait_ge(acol_done, 1)
                    if k == 0:
                        evacuate(v, s["q"], ACT.Silu, bias=b_in(col))
                    elif k in (1, 2):
                        nc.scalar.activation(s[f"f{k - 1}"], bank[v % 2][:], ACT.Sigmoid,
                                             bias=b_in(col)).then_inc(sig_done, 1)
                        evacuate(v, s[f"k{k - 1}"], ACT.Sigmoid, bias=neg_b_in[:, col:col + 1], scale=-1.0)
                    elif k == 3:
                        if h > 0:
                            act.wait_ge(vT_done, 2 + h)
                        evacuate(v, gate_in[0][:], ACT.Identity, bias=b_in(col))
                    else:
                        evacuate(v, s["g"], ACT.Silu, bias=b_in(col))
                else:
                    h, k = divmod(v - V_ML, 4)
                    s = ml[h % 2]
                    col = 20 + 4 * k + h
                    act.wait_ge(unit_done, v + 1)
                    if h == 0 and k == 0:
                        act.wait_ge(pad_done, 4)
                    if h >= 2 and k == 0:
                        act.wait_ge(op_ready, J_Y2 + 4 + h - 1)
                    if k < 2:
                        evacuate(v, s["qk"[k]][:, 2:2 + S], ACT.Identity, bias=b_in(col))
                    elif k == 2:
                        act.wait_ge(vT_done, 2 + NH2 + h)
                        evacuate(v, gate_in[0][:], ACT.Identity, bias=b_in(col))
                    else:
                        evacuate(v, s["o"], ACT.Sigmoid, bias=b_in(col))

            def head_square(src):
                nc.scalar.activation(square[0][:], src, ACT.Square).then_inc(hsq_done, 1)

            def head_rstd(h):
                act.wait_ge(hsum_done, h + 1)
                nc.scalar.activation(rstd[:], bank[4][:], ACT.Ln, bias=eps_col[:, 0:1], scale=1.0 / P).then_inc(hln_done, 1)
                act.wait_ge(hln_done, h + 1)
                nc.scalar.activation(rstd[:], rstd[:], ACT.Exp, scale=-0.5).then_inc(hrs_done, 1)

            def head_hi(h):
                act.wait_ge(op_src, h + 1)
                nc.scalar.activation(ghi[:, h, :], opnd[h % 2][:], ACT.Copy).then_inc(op_hi, 1)

            for k in range(5):
                group_unit(V_HG + k)
            for kind, h, units in unit_groups():
                if kind == "hg":
                    for k, v in enumerate(units):
                        group_unit(v)
                        if h > 0 and k == 0:
                            head_rstd(h - 1)
                        if h > 0 and k == 1:
                            head_hi(h - 1)
                    act.wait_ge(o2_done, h + 1)
                    head_square(bank[6][:])
                    if h == NH2 - 1:
                        head_rstd(h)
                        head_hi(h)
                    continue
                units = list(units)
                for k in range(4):
                    act.wait_ge(bc_done, 4 * h + k + 1)
                    dst, func = (neg_m[k], ACT.Copy) if k < 2 else (em[k - 2], ACT.Exp)
                    if h > 0 and k == 0:
                        act.wait_ge(ml_step, ML_STEPS * h)
                    nc.scalar.activation(dst, bank[5][:], func).then_inc(bc_out, 1)
                if h > 0:
                    head_rstd(NH2 + h - 1)
                for k in range(2):
                    act.wait_ge(tap_done, 10 * h + 5 * k + 5)
                    nc.scalar.activation((ml_q, ml_k)[k], dmat[k], ACT.Silu,
                                         bias=vcol("mconv_b", 4 * k + h)).then_inc(qk_done, 1)
                if h > 0:
                    head_hi(NH2 + h - 1)
                if units:
                    group_unit(units.pop(0))
                for y in range(2 * NB):
                    b, dr = divmod(y, 2)
                    t0, t1, _ = s_range(dr, b)
                    act.wait_ge(d_arg, 8 * h + y + 1)
                    nc.scalar.activation(dmat[dr][:, t0:t1], dmat[dr][:, t0:t1], ACT.Exp).then_inc(d_exp, 1)
                    if y > 1 and y % 2 == 1 and units:
                        group_unit(units.pop(0))
                for dr in range(2):
                    act.wait_ge(nd_done, 2 * h + dr + 1)
                    nc.scalar.activation(dmat[dr], bank[(5, 3)[dr]][:], ACT.Abs).then_inc(abs_done, 1)
                act.wait_ge(ml_step, ML_STEPS * (h + 1))
                head_square(ml_h[0])
                if h == NH2 - 1:
                    head_rstd(NH2 + h)
                    head_hi(NH2 + h)

            for c in range(DC):
                split_next(V_WO2 + c)
            norm_stats(N_MEM)
            norm_hi(N_MEM, V_WO2)
            for c in range(DC):
                v = V_XK + c
                split_next(v)
                act.wait_ge(unit_done, v + 1)
                evacuate(v, xk[:, c, :], ACT.Copy, n=MEM)
            for c in range(DC):
                v = V_XV + c
                split_next(v)
                act.wait_ge(unit_done, v + 1)
                if c >= 2:
                    act.wait_ge(vT_done, 10 + c - 1)
                evacuate(v, x_vT[c % 2], ACT.Copy, n=MEM)
            norm_stats(N_XATTN)
            norm_hi(N_XATTN, V_XQ)
            for c in range(DC + 4):
                v = V_XQ + c
                if c < DC:
                    split_next(v)
                    act.wait_ge(unit_done, v + 1)
                    evacuate(v, xq[:, c, :], ACT.Copy)
                if c >= 2 and c % 2 == 0 and c < DC + 2:
                    step_exp(16 + c // 2 - 1, x_prob, 0, False)
                if c >= 3 and c % 2 == 1 and c < DC + 3:
                    step_turned(16 + (c - 3) // 2, x_probT, range(2))
                if c >= 5 and c % 2 == 1:
                    act.wait_ge(pv_out, 16 + (c - 5) // 2 + 1)
                    for e in range(2):
                        nc.scalar.activation(ghi[:, c - 5 + e, :], xq[:, c - 5 + e, :], ACT.Copy).then_inc(op_hi, 1)
            for c in range(DC):
                split_next(V_XO + c)
                if c > 0:
                    norm_square(N_MLP, c - 1)
            norm_stats(N_MLP, DC - 1)
            norm_hi(N_MLP)

            def mlp(i, last):
                for c in range(DC):
                    v = V_MLP + c
                    split(v + 1, 4 * i, raw_of(v + 1), 4 * i)
                    act.wait_ge(unit_done, v + 1 + 16 * i)
                    nc.scalar.activation(gate_in[c % 2][:], bank[v % 2][:], ACT.Relu).then_inc(evac[v % 2], 1)
                    act.wait_ge(op_src, 8 + c + 1 + DC * i)
                    nc.scalar.activation(ghi[:, c, :], opnd[c % 2][:], ACT.Copy).then_inc(op_hi, 1)
                for c in range(DC):
                    v = V_MLP + DC + c
                    if c < DC - 1 or not last:
                        split(v + 1, 4 * i, raw_of(v + 1), 4 * i)
                    if last and c > 0:
                        norm_square(N_OUT, c - 1)

            with act.Fori(0, MLP_PARTS - 1) as i:
                mlp(i, False)
            mlp(MLP_PARTS - 1, True)
            norm_stats(N_OUT, DC - 1)
            for c in range(DC):
                act.wait_ge(normed_done, DC * N_OUT + c + 1)
                act.dma_start(out[:, c, :], xT[:, c, :]).then_inc(stored, 16)

        @block.vector
        def _(dve):
            nxt = [0]

            def split(v, dv=0):
                kc = chunks_of(v)
                u = raw_of(v)
                dve.wait_ge(w_hi, v + 1 + 4 * dv)
                nc.vector.tensor_tensor(wlo[v % 2][:, 0:kc * P], raw[u % 4][:, 0:kc * P],
                                        whi[v % 2][:, 0:kc * P].bitcast(F32), ALU.subtract).then_inc(w_split, 1)

            def split_next(v):
                if nxt[0] <= v + 1 < V_END:
                    split(v + 1)
                    nxt[0] = v + 2

            def stt(out_ap, in0, scalar, in1, op0, op1):
                return nc.vector.scalar_tensor_tensor(out=out_ap, in0=in0, scalar=scalar, in1=in1, op0=op0, op1=op1)

            def norm(n):
                w = width(n)
                dve.wait_ge(rstd_done, n + 1)

                def rest(c):
                    dve.wait_ge(h_hi, H_AT[n] + c + 1)
                    hi, lo = h_out(n, c)
                    stt(lo, normed[c % 2][:, 0:w], shift(n, c), hi.bitcast(F32), ALU.add,
                        ALU.subtract).then_inc(h_ready, 1)

                for c in range(DC):
                    if n in H_AT:
                        if c >= 2:
                            rest(c - 2)
                        if H_AT[n] + c >= 2:
                            dve.wait_ge(h_ready, H_AT[n] + max(c - 1, 0))
                        dst = normed[c % 2][:, 0:w]
                    else:
                        dst = xT[:, c, :]
                    stt(dst, norm_src(n, c), gscale[:, n * DC + c:n * DC + c + 1], rstd[:, 0:w], ALU.mult,
                        ALU.mult).then_inc(normed_done, 1)
                if n in H_AT:
                    rest(DC - 2)
                    rest(DC - 1)

            def operand_lo(j, c, src=None, bufs=None):
                hi, lo = bufs or (ghi, glo)
                dve.wait_ge(op_hi, j + 1)
                nc.vector.tensor_tensor(lo[:, c, :], opnd[j % 2][:] if src is None else src,
                                        hi[:, c, :].bitcast(F32), ALU.subtract).then_inc(op_ready, 1)

            def residual(v, c, scale=None, dv=0):
                dve.wait_ge(unit_done, v + 1 + 4 * dv)
                if scale is None:
                    ins = nc.vector.tensor_tensor(xT[:, c, :], bank[v % 2][:], xT[:, c, :], ALU.add)
                else:
                    ins = stt(xT[:, c, :], bank[v % 2][:], scale, xT[:, c, :], ALU.mult, ALU.add)
                ins.then_inc(evac[v % 2], 1)

            def ada(a, da=0):
                u, acc = raw_of_ada(a), ada_acc[a % 4]
                straight = isinstance(da, int)
                dve.wait_ge(landed[u % 4], 16 * (u // 4 + 1) + (4 if a < ADA_HEAD_N else 8) * da)
                if a >= 4 or not straight:
                    dve.wait_ge(ada_done, a - 3 + da)
                for c in range(DC):
                    w = raw[u % 4][:, c * P:(c + 1) * P]
                    if c == 0:
                        ins = nc.vector.tensor_scalar(acc, w, cact[:, 0:1], None, ALU.mult)
                    else:
                        dve.wait_ge(ada_step, DC * a + c + DC * da)
                        ins = stt(acc, w, cact[:, c:c + 1], acc, ALU.mult, ALU.add)
                    ins.then_inc(ada_step, 1)

            def take_mods(a0, a1, upto=None):
                dve.wait_ge(ada_done, upto or a1)
                nc.vector.tensor_tensor(mods[:, a0:a1], bank[7][:, a0:a1], vec[:, VEC["b_ada"] + a0:VEC["b_ada"] + a1],
                                        ALU.add).then_inc(mods_done, 1)

            def swiglu(f):
                base, j0 = V_FFN[f], J_FFN[f]
                for part, kc in enumerate(FF_PARTS):
                    v0, j1 = base + 24 * part, j0 + 8 * part

                    def body(i, last):
                        for k in range(2):
                            v, j = v0 + 2 * k, j1 + k
                            split(v + 1, i)
                            if f == 0:
                                ada(ADA_PART[part] + 2 * k, 4 * i)
                            if k == 0:
                                split(v + 2, i)
                            elif not last:
                                split(v0, i + 1)
                            else:
                                split(v + 2 + 4 * i)
                            if f == 0:
                                ada(ADA_PART[part] + 2 * k + 1, 4 * i)
                            dve.wait_ge(evac[0], v // 2 + 1 + 2 * i)
                            dve.wait_ge(unit_done, v + 2 + 4 * i)
                            if j >= 2 or not isinstance(i, int) or i > 0:
                                dve.wait_ge(op_ready, j - 1 + 2 * i)
                            nc.vector.tensor_tensor(opnd[k][:], bank[1][:], gate_in[k][:], ALU.mult).then_inc(evac[1], 1)
                            dve.wait_ge(op_hi, j + 1 + 2 * i)
                            if isinstance(i, int):
                                g = slice(2 * i + k, 2 * i + k + 1)
                            else:
                                g = bass.ds(2 * i + k, 1)
                            nc.vector.tensor_tensor(glo[:, g, :], opnd[k][:].unsqueeze(1), ghi[:, g, :].bitcast(F32),
                                                    ALU.subtract).then_inc(op_ready, 1)

                    body(0, False)
                    with dve.Fori(1, kc // 2 - 1) as i:
                        body(i, False)
                    body(kc // 2 - 1, True)
                    if f == 0 and part == 0:
                        take_mods(2 * DC, 3 * DC, ADA_PART[0] + 2 * kc)
                        dve.wait_ge(mods_done, 4)
                        nc.vector.tensor_scalar(mods[:, 2 * DC:3 * DC], mods[:, 2 * DC:3 * DC], 0.5, None,
                                                ALU.mult).then_inc(mods_done, 1)
                        dve.wait_ge(mods_done, 5)
                    v = v0 + 2 * kc
                    for c in range(DC):
                        split(v + c + 1)
                        residual(v + c, c, mod(2 if f == 0 else 8, c))
                        if f == 0 and c < ADA_TAIL:
                            ada(ADA_PART[part + 1] - ADA_TAIL + c)
                    if f == 0:
                        take_mods(max(3 * DC, ADA_PART[part]), ADA_PART[part + 1])
                nxt[0] = base + V_FFN_LEN + 1

            for t, val in ((zero_col, 0.0), (eps_col, EPS)):
                nc.vector.memset(t[:], val)
            dve.wait_ge(small_in, 16)
            lbv = vec[:, VEC["lb"]:VEC["lb"] + 8]
            nc.vector.tensor_tensor(lbt[:, 0, :], lbv, lbv, ALU.subtract).then_inc(setup_v, 1)
            nc.vector.tensor_scalar(neg_b_in[:], vec[:, VEC["b_in"]:VEC["b_in"] + 36], -1.0, None, ALU.mult)
            nc.vector.tensor_scalar(neg_sink[:], vec[:, VEC["sinks"]:VEC["sinks"] + N_Q], -1.0, None,
                                    ALU.mult).then_inc(setup_v, 1)
            dve.wait_ge(setup_a, 1)
            nc.vector.reciprocal(lbt[:, 2, :], lbt[:, 1, :]).then_inc(setup_v, 1)
            dve.wait_ge(setup_v, 3)
            nc.vector.tensor_tensor(lbt[:, 0, :], lbt[:, 1, :], lbt[:, 2, :], ALU.mult).then_inc(setup_v, 1)
            dve.wait_ge(setup_v, 4)
            nc.vector.tensor_tensor(lbs[:, 0, :], lbt[:, 0, :], lbt[:, 0, :], ALU.subtract).then_inc(setup_v, 1)
            dve.wait_ge(setup_v, 5)
            nc.vector.tensor_scalar(lbs[:, 1, :], lbs[:, 0, :], -1.0, 1.0, ALU.mult, ALU.add).then_inc(setup_v, 1)
            gain = vec[:, VEC["gain"]:VEC["gain"] + 9 * DC]
            nc.vector.tensor_copy(gscale[:], gain).then_inc(mods_done, 1)
            dve.wait_ge(cact_ready, 1)
            for a in range(4):
                ada(a)
            with dve.Fori(1, ADA_HEAD_N // 4) as i:
                for a in range(4):
                    ada(a, 4 * i)
            take_mods(0, ADA_HEAD_N)
            dve.wait_ge(mods_done, 2)
            stt(gscale[:, 0:DC], mods[:, DC:2 * DC], 1.0, gain[:, 0:DC], ALU.add, ALU.mult).then_inc(mods_done, 1)
            dve.wait_ge(mods_done, 3)
            norm(N_FFN1)
            split(0)
            swiglu(0)
            dve.wait_ge(mods_done, 8)
            for n in (N_MIX, N_FFN2):
                k = SH[n] + 1
                stt(gscale[:, n * DC:(n + 1) * DC], mods[:, k * DC:(k + 1) * DC], 1.0, gain[:, n * DC:(n + 1) * DC],
                    ALU.add, ALU.mult).then_inc(mods_done, 1)
            nc.vector.tensor_scalar(mods[:, 8 * DC:], mods[:, 8 * DC:], 0.5, None, ALU.mult).then_inc(mods_done, 1)
            dve.wait_ge(mods_done, 11)
            dve.wait_ge(mask_landed, 16)
            dve.wait_ge(con_landed, 16)
            nc.vector.tensor_copy(level_mask[:], mask_f32).then_inc(pad_done, 1)

            norm(N_MIX)
            for i in range(2):
                nc.vector.memset(conv_in[i][:, 0:2], 0.0).then_inc(pad_done, 1)
            dve.wait_ge(rope_in_s, 16)
            for j in range(10):
                v = V_MIX + j
                split_next(v)
                ra, rb = rope_a[:, 0:2, :].rearrange("p a b -> p (a b)"), rope_b[:, 0:2, :].rearrange("p a b -> p (a b)")
                dve.wait_ge(evac[v % 2], v // 2 + 1)
                if j > 0:
                    dve.wait_ge(rope_done, j)
                nc.vector.tensor_tensor(ra, gate_in[j % 2][:], rope[:, 0, :], ALU.mult).then_inc(rope_mul, 1)
                split_next(v + 1)
                dve.wait_ge(rot_done, j + 1)
                nc.vector.tensor_tensor(rb, bank[2 + j % 2][:], rope[:, 1, :], ALU.mult).then_inc(rope_mul, 1)
                dve.wait_ge(rope_mul, 2 * j + 2)
                dst = qT[:, j, :] if j < DC else kT[:, j - DC, :]
                nc.vector.tensor_tensor(dst, ra, rb, ALU.add).then_inc(rope_done, 1)
            for t in range(2):
                split_next(V_MIX + 10 + t)
                dve.wait_ge(vT_done, t + 1)
                nc.vector.tensor_copy(v_tok[:, :, t * P:(t + 1) * P],
                                      bank[4 + t][:].rearrange("p (a b) -> p a b", b=P)).then_inc(vtok_done, 1)

            def softmax_first(i, S_, lo, sink, scale):
                p = i % 2
                dve.wait_ge(score_done, i + 1)
                if i == 0:
                    dve.wait_ge(rope_done, 10)
                if i >= 2:
                    dve.wait_ge(turned, i - 1)
                for a in range(2):
                    src = bank[2 + a][:].rearrange("p (h k) -> p h k", k=2 * P)[:, :, lo:]
                    dst = S_[p][:, 2 * a:2 * a + 2, lo:]
                    if sink:
                        mask = win[:, lo:].unsqueeze(1).to_broadcast([P, 2, 2 * P - lo])
                        stt(dst, src, scale, mask, ALU.mult, ALU.add).then_inc(masked, 1)
                    else:
                        nc.vector.tensor_scalar(dst, src, scale, None, ALU.mult).then_inc(masked, 1)
                dve.wait_ge(masked, 2 * i + 2)
                nc.vector.tensor_reduce(stat[:, p, ROW_MAX, :], S_[p][:, :, lo:], AX_X, ALU.max).then_inc(row_max, 1)
                dve.wait_ge(row_max, i + 1)
                if sink:
                    g = i // 4
                    stt(stat[:, p, NEG_MAX, :], stat[:, p, ROW_MAX, :], -1.0, neg_sink[:, 4 * g:4 * g + 4], ALU.mult,
                        ALU.min).then_inc(neg_max, 1)
                    dve.wait_ge(neg_max, i + 1)
                    nc.vector.tensor_tensor(stat[:, p, SINK, :], stat[:, p, NEG_MAX, :],
                                            vec[:, VEC["sinks"] + 4 * g:VEC["sinks"] + 4 * g + 4],
                                            ALU.add).then_inc(sink_sum, 1)
                else:
                    nc.vector.tensor_scalar(stat[:, p, NEG_MAX, :], stat[:, p, ROW_MAX, :], -1.0, None,
                                            ALU.mult).then_inc(neg_max, 1)

            def softmax_last(i, S_, lo, sink):
                p = i % 2
                dve.wait_ge(exp_done, i + 1)
                den = stat[:, p, SUM, :]
                if sink:
                    nc.vector.tensor_tensor(stat[:, p, DEN, :], den, stat[:, p, SINK, :], ALU.add).then_inc(den_done, 1)
                    dve.wait_ge(den_done, i + 1)
                    den = stat[:, p, DEN, :]
                nc.vector.reciprocal(stat[:, p, RDEN, :], den).then_inc(rden_done, 1)
                dve.wait_ge(rden_done, i + 1)
                for hh in range(4):
                    ins = nc.vector.tensor_scalar(S_[p][:, hh, lo:], S_[p][:, hh, lo:], stat[:, p, RDEN, hh:hh + 1], None,
                                                  ALU.mult)
                ins.then_inc(prob_done, 1)

            def take_output(i):
                g, n = divmod(i, 4)
                half = (g % 2) * HD
                dve.wait_ge(pv_done, i + 1)
                nc.vector.tensor_copy(qT[half:half + HD, 4 * (g // 2):4 * (g // 2) + 4, n * P:(n + 1) * P],
                                      bank[6][0:HD, :].rearrange("p (h q) -> p h q", q=P)).then_inc(pv_out, 1)

            def conv_unit(v):
                c, k = divmod(v - V_CONV, 3)
                split_next(v)
                cin = conv_in[c % 2]
                if k == 1:
                    dve.wait_ge(evac[(v - 1) % 2], (v - 1) // 2 + 1)
                    dve.wait_ge(unit_done, v + 1)
                    nc.vector.tensor_tensor(cin[:, 2:], bank[v % 2][:], gate_in[c % 2][:], ALU.mult).then_inc(evac[v % 2], 1)
                    dve.wait_ge(evac[v % 2], v // 2 + 1)
                    for tap in range(3):
                        src = cin[:, 2 - tap:2 - tap + S]
                        w = vcol("conv_w", DC * (2 - tap) + c)
                        if tap == 0:
                            ins = nc.vector.tensor_scalar(conv_out, src, w, None, ALU.mult)
                        else:
                            dve.wait_ge(conv_step, 3 * c + tap)
                            ins = stt(conv_out, src, w, conv_out, ALU.mult, ALU.add)
                        ins.then_inc(conv_step, 1)
                if k == 2:
                    dve.wait_ge(unit_done, v + 1)
                    dve.wait_ge(conv_step, 3 * c + 3)
                    dve.wait_ge(op_ready, J_Y + c - 1)
                    nc.vector.tensor_tensor(opnd[c % 2][:], bank[v % 2][:], conv_out, ALU.mult).then_inc(evac[v % 2], 1)
                    operand_lo(J_Y + c, c)

            def gate_unit(v, base):
                c, k = divmod(v - base, 2)
                split_next(v)
                if k == 1:
                    dve.wait_ge(evac[(v - 1) % 2], (v - 1) // 2 + 1)
                    dve.wait_ge(unit_done, v + 1)
                    if base == V_CP:
                        nc.vector.tensor_tensor(merged[:, c, :], bank[v % 2][:], gate_in[c % 2][:],
                                                ALU.mult).then_inc(evac[v % 2], 1)
                    else:
                        nc.vector.tensor_tensor(conv_out, bank[v % 2][:], gate_in[c % 2][:],
                                                ALU.mult).then_inc(evac[v % 2], 1)
                        dve.wait_ge(evac[v % 2], v // 2 + 1)
                        nc.vector.tensor_tensor(merged[:, c, :], merged[:, c, :], conv_out, ALU.add).then_inc(gated, 1)

            for i in range(16):
                units = slot_units(i)
                lo = 0 if i % 4 else P
                for a, v in enumerate(units):
                    if a == 1:
                        split_next(v)
                        softmax_last(i, prob, lo, True)
                    (conv_unit if v < V_CP else lambda u: gate_unit(u, V_CP))(v)
                    if a == 0:
                        softmax_first(i, prob, lo, True, SCORE_SCALE)
                        if i > 1:
                            take_output(i - 2)
            take_output(14)
            take_output(15)
            for c in range(DC):
                if c == 0:
                    dve.wait_ge(pv_out, 16)
                operand_lo(J_O + c, c, src=qT[:, c, :])
            for c in range(2 * DC):
                gate_unit(V_AP + c, V_AP)
            for c in range(DC):
                operand_lo(J_M + c, c, src=merged[:, c, :], bufs=(hhi, hlo))
            for c in range(DC):
                split_next(V_WO + c)
                residual(V_WO + c, c, mod(5, c))
            norm(N_FFN2)
            swiglu(1)

            norm(N_FINAL)
            norm(N_MIX2)
            split_next(V_GATE)
            for dr in range(2):
                for t in "qk":
                    for cols in (slice(0, 2), slice(S + 2, S + 4)):
                        ins = nc.vector.memset(ml[dr][t][:, cols], 0.0)
            ins.then_inc(pad_done, 1)
            dve.wait_ge(gate_chain, 4)
            dve.wait_ge(evac[V_GATE % 2], V_GATE // 2 + 1)
            R = {k: t[0:8, :] for k, t in row.items()}
            chain = [4]

            def link(ins):
                chain[0] += 1
                ins.then_inc(gate_chain, 1)
                dve.wait_ge(gate_chain, chain[0])

            link(stt(R["lf"], R["z"], 0.0, R["t"], ALU.min, ALU.subtract))
            for dr in range(2):
                rev = (lambda t: t) if dr == 0 else (lambda t: t[:, ::-1])
                a_row = R["a"] if dr == 0 else R["z"]
                link(nc.vector.tensor_tensor_scan(rev(R[f"cum{dr}"]), rev(R["lf"]), rev(R["lf"]), 0.0, ALU.add, ALU.bypass))
                link(nc.vector.tensor_tensor(a_row, R["ig"], R[f"cum{dr}"], ALU.subtract))
                link(nc.vector.tensor_tensor_scan(rev(R["t"]), rev(a_row), rev(a_row), 0.0, ALU.max, ALU.max))
                nc.vector.tensor_scalar(gate_rows[32 * dr:32 * dr + 8, :], R["t"], -1.0, None, ALU.mult)
                link(stt(gate_rows[64 + 32 * dr:72 + 32 * dr, :], R["t"], -1.0, R[f"cum{dr}"], ALU.mult, ALU.subtract))

            def group_unit(v):
                split_next(v)
                if v < V_ML:
                    h, k = divmod(v - V_HG, 5)
                    s = hg[h % 2]
                    if k in (1, 2):
                        d = k - 1
                        col = 4 * d + h
                        dve.wait_ge(sig_done, 2 * h + d + 1)
                        nc.vector.tensor_scalar(s[f"f{d}"], s[f"f{d}"], lbs[:, 1, col:col + 1], lbs[:, 0, col:col + 1],
                                                ALU.mult, ALU.add).then_inc(fk_done, 1)
                        dve.wait_ge(evac[v % 2], v // 2 + 1)
                        nc.vector.tensor_scalar(s[f"k{d}"], s[f"k{d}"], lbs[:, 1, col:col + 1], None,
                                                ALU.mult).then_inc(fk_done, 1)
                    if k == 3:
                        dve.wait_ge(vT_done, 2 + h + 1)
                        nc.vector.tensor_copy(s["v"], bank[5][:]).then_inc(vtok_done, 1)
                else:
                    h, k = divmod(v - V_ML, 4)
                    if k == 2:
                        dve.wait_ge(vT_done, 2 + NH2 + h + 1)
                        nc.vector.tensor_copy(ml[h % 2]["v"], bank[4][:]).then_inc(vtok_done, 1)

            def head_out(h, src, gname, gate):
                dve.wait_ge(hrs_done, h + 1)
                stt(normed[0][:], src, vcol(gname, h % NH2), rstd[:], ALU.mult, ALU.mult).then_inc(hnorm_t, 1)
                dve.wait_ge(hnorm_t, h + 1)
                nc.vector.tensor_tensor(opnd[h % 2][:], normed[0][:], gate, ALU.mult).then_inc(op_src, 1)

            def hg_out(h):
                vg = V_HG + 5 * h + 4
                dve.wait_ge(evac[vg % 2], vg // 2 + 1)
                dve.wait_ge(o2_done, h + 1)
                head_out(h, bank[6][:], "hgrn_g", hg[h % 2]["g"])

            def ml_out(h):
                vo = V_ML + 4 * h + 3
                dve.wait_ge(evac[vo % 2], vo // 2 + 1)
                head_out(NH2 + h, ml_h[0], "mlstm_g", ml[h % 2]["o"])

            def update(h, s, m, dr):
                f = fsrc(s, dr, m)
                fp = f.rearrange("p (j a) -> p j a", a=2)
                n, blk = S >> (m + 1), 1 << m
                qq = pairs(q_fwd if dr == 0 else s["q"], blk)
                kk = pairs(s[f"k{dr}"], blk)
                late = 1 - dr
                if m < LEVELS:
                    nc.vector.tensor_tensor(fsrc(s, dr, m + 1).unsqueeze(2), fp[:, :, 0:1], fp[:, :, 1:2], ALU.mult)
                nc.vector.tensor_tensor(qq[:, :, late, :], qq[:, :, late, :],
                                        fp[:, :, 1 - late:2 - late].to_broadcast([P, n, blk]), ALU.mult)
                nc.vector.tensor_tensor(kk[:, :, 1 - late, :], kk[:, :, 1 - late, :],
                                        fp[:, :, late:late + 1].to_broadcast([P, n, blk]), ALU.mult).then_inc(decay, 1)

            def hg_items(h, zs):
                s = hg[h % 2]
                for z in zs:
                    dve.wait_ge(lev_done, ITEMS * h + z + 1)
                    b = bank[2 + z % 2][:]
                    b3 = b.rearrange("p (a t) -> p a t", t=P)
                    if z == 0:
                        nc.vector.tensor_tensor(diag, b3, ident.unsqueeze(1).to_broadcast([P, NB, P]),
                                                ALU.mult).then_inc(lev_taken, 1)
                        dve.wait_ge(fk_done, 4 * h + 4)
                        nc.vector.tensor_tensor(s["q"], s["q"], s["f1"], ALU.mult).then_inc(decay, 1)
                    elif z <= 2 * LEVELS:
                        m, dr = divmod(z - 1, 2)
                        dve.wait_ge(lev_taken, ITEMS * h + z)
                        nc.vector.copy_predicated(diag, level_mask[:, 2 * m + dr, :].unsqueeze(1).to_broadcast([P, NB, P]),
                                                  b3).then_inc(lev_taken, 1)
                        dve.wait_ge(decay, EVENTS * h + (2 + dr if m == 0 else 4 + dr + 2 * (m - 1)))
                        update(h, s, m, dr)
                    elif z == 2 * LEVELS + 1:
                        for k, (sb_, tb) in enumerate(((0, 1), (2, 3), (1, 0), (3, 2))):
                            ins = nc.vector.tensor_copy(scT[:, sb_ * S + tb * P:sb_ * S + (tb + 1) * P], b3[:, k, :])
                        ins.then_inc(lev_taken, 1)
                        for dr in range(2):
                            dve.wait_ge(decay, EVENTS * h + 4 + dr + 2 * (LEVELS - 1))
                            update(h, s, LEVELS, dr)
                    else:
                        dr = z - 2 * LEVELS - 2
                        for k in range(2):
                            sb_ = (0, 2)[dr] + k
                            t0 = (S // 2, 0)[dr]
                            ins = nc.vector.tensor_copy(scT[:, sb_ * S + t0:sb_ * S + t0 + S // 2],
                                                        b[:, k * S // 2:(k + 1) * S // 2])
                        ins.then_inc(lev_taken, 1)

            for k in range(5):
                group_unit(V_HG + k)
            dve.wait_ge(acol_done, 1)
            nc.vector.tensor_copy(acol[:].rearrange("p a b c -> p (a b c)"), bank[3][:, 0:64]).then_inc(acol_done, 1)
            for kind, h, units in unit_groups():
                units = list(units)
                if kind == "hg":
                    s = hg[h % 2]
                    vq = V_HG + 5 * h
                    dve.wait_ge(evac[vq % 2], vq // 2 + 1)
                    dve.wait_ge(fk_done, 4 * h + 4)
                    nc.vector.tensor_tensor(normed[1][:], s["k0"], s["k1"], ALU.add).then_inc(decay, 1)
                    if h > 0:
                        dve.wait_ge(lev_done, ITEMS * h)
                    nc.vector.tensor_tensor(q_fwd, s["q"], s["f0"], ALU.mult).then_inc(decay, 1)
                    for sl in range(5):
                        if units:
                            group_unit(units.pop(0))
                        if sl == 0 and h > 0:
                            dve.wait_ge(o2_done, h)
                        hg_items(h, ITEM_SLOTS[sl])
                        if sl == 0 and h > 0:
                            hg_out(h - 1)
                        if sl == 1 and h > 0:
                            operand_lo(J_Y2 + h - 1, h - 1)
                    if h == NH2 - 1:
                        hg_out(h)
                        operand_lo(J_Y2 + h, h)
                    continue
                s = ml[h % 2]
                for k, t in enumerate("qk"):
                    v = V_ML + 4 * h + k
                    dve.wait_ge(evac[v % 2], v // 2 + 1)
                    if h > 0:
                        dve.wait_ge(abs_done, 2 * h)
                    else:
                        dve.wait_ge(op_ready, J_Y2 + NH2)
                    for tap in range(5):
                        w = vcol("mconv_w", DC * tap + 4 * k + h)
                        src = s[t][:, tap:tap + S]
                        if tap == 0:
                            ins = nc.vector.tensor_scalar(dmat[k], src, w, None, ALU.mult)
                        else:
                            dve.wait_ge(tap_done, 10 * h + 5 * k + tap)
                            ins = stt(dmat[k], src, w, dmat[k], ALU.mult, ALU.add)
                        ins.then_inc(tap_done, 1)
                if h > 0:
                    ml_out(h - 1)
                    operand_lo(J_Y2 + NH2 + h - 1, NH2 + h - 1)
                if units:
                    group_unit(units.pop(0))

                def arg(y):
                    b, dr = divmod(y, 2)
                    t0, t1, _ = s_range(dr, b)
                    if y >= 2:
                        dve.wait_ge(s_mul, 8 * h + y - 1)
                    nc.vector.tensor_scalar(dmat[dr][:, t0:t1], neg_m[dr][:, t0:t1], acol[:, dr, b, 4 * dr + h:4 * dr + h + 1],
                                            0.0, ALU.add, ALU.min).then_inc(d_arg, 1)

                dve.wait_ge(qk_done, 2 * h + 2)
                dve.wait_ge(bc_out, 4 * h + 2)
                if h == 0:
                    dve.wait_ge(acol_done, 2)
                else:
                    dve.wait_ge(nd_done, 2 * h)
                arg(0)
                for y in range(2 * NB):
                    b, dr = divmod(y, 2)
                    t0, t1, at_ = s_range(dr, b)
                    if y + 1 < 2 * NB:
                        arg(y + 1)
                    dve.wait_ge(pair_done, NB * h + b + 1)
                    dve.wait_ge(d_exp, 8 * h + y + 1)
                    stt(sT[dr][:, at_:at_ + t1 - t0], bank[2 + b % 2][:, t0:t1], MLSTM_SCALE, dmat[dr][:, t0:t1],
                        ALU.mult, ALU.mult).then_inc(s_mul, 1)
                    dve.wait_ge(s_mul, 8 * h + y + 1)
                    d = at_ + b * P - t0
                    nc.vector.tensor_tensor(sT[dr][:, d:d + P], sT[dr][:, d:d + P], tri[:, dr, :], ALU.mult).then_inc(s_done, 1)
                    if y > 1 and y % 2 == 1 and units:
                        group_unit(units.pop(0))
                n_ = [ML_STEPS * h]

                def step(ins):
                    n_[0] += 1
                    ins.then_inc(ml_step, 1)
                    dve.wait_ge(ml_step, n_[0])

                for dr in range(2):
                    dve.wait_ge(abs_done, 2 * h + dr + 1)
                    dve.wait_ge(bc_out, 4 * h + 3 + dr)
                    step(nc.vector.tensor_tensor(dmat[dr], dmat[dr], em[dr], ALU.max))
                    step(nc.vector.reciprocal(ml_h[dr], dmat[dr]))
                    step(nc.vector.tensor_tensor(ml_h[dr], bank[6 + dr][:], ml_h[dr], ALU.mult))
                step(nc.vector.tensor_tensor(ml_h[0], ml_h[0], ml_h[1], ALU.add))
                if h == NH2 - 1:
                    ml_out(h)
                    operand_lo(J_Y2 + NH2 + h, NH2 + h)

            for c in range(DC):
                split_next(V_WO2 + c)
                residual(V_WO2 + c, c)
            norm(N_MEM)
            for c in range(DC):
                split_next(V_XK + c)
            for c in range(DC):
                split_next(V_XV + c)
                dve.wait_ge(vT_done, 10 + c + 1)
                nc.vector.tensor_copy(xv[:, :, c * P:(c + 1) * P],
                                      bank[6 + c % 2][:, 0:MEM].rearrange("p (a b) -> p a b", b=P)).then_inc(vtok_done, 1)
            norm(N_XATTN)
            def x_output(hh):
                dve.wait_ge(pv_done, 16 + hh + 1)
                for e in range(2):
                    nc.vector.tensor_copy(xq[:, 2 * hh + e, :], bank[6 + e][:]).then_inc(pv_out if e else x_half, 1)

            for c in range(DC + 4):
                if c < DC:
                    split_next(V_XQ + c)
                if c >= 2 and c % 2 == 0 and c < DC + 2:
                    softmax_first(16 + c // 2 - 1, x_prob, 0, False, XATTN_SCALE)
                if c >= 2 and c % 2 == 0 and c < DC + 2:
                    softmax_last(16 + c // 2 - 1, x_prob, 0, False)
                if c >= 5 and c % 2 == 1:
                    x_output((c - 5) // 2)
                    for e in range(2):
                        dve.wait_ge(pv_out, 16 + (c - 5) // 2 + 1)
                        operand_lo(J_XO + c - 5 + e, c - 5 + e, src=xq[:, c - 5 + e, :])
            for c in range(DC):
                split_next(V_XO + c)
                residual(V_XO + c, c)
            norm(N_MLP)

            def mlp(i, last):
                for c in range(DC):
                    v = V_MLP + c
                    split(v + 1, 4 * i)
                    dve.wait_ge(evac[v % 2], v // 2 + 1 + 8 * i)
                    dve.wait_ge(op_ready, J_MLP + c - 1 + DC * i)
                    nc.vector.tensor_tensor(opnd[c % 2][:], gate_in[c % 2][:], gate_in[c % 2][:], ALU.mult).then_inc(op_src, 1)
                    dve.wait_ge(op_hi, J_MLP + c + 1 + DC * i)
                    nc.vector.tensor_tensor(glo[:, c, :], opnd[c % 2][:], ghi[:, c, :].bitcast(F32),
                                            ALU.subtract).then_inc(op_ready, 1)
                for c in range(DC):
                    v = V_MLP + DC + c
                    if c < DC - 1 or not last:
                        split(v + 1, 4 * i)
                    residual(v, c, dv=4 * i)

            with dve.Fori(0, MLP_PARTS - 1) as i:
                mlp(i, False)
            mlp(MLP_PARTS - 1, True)
            norm(N_OUT)

        @block.tensor
        def _(pe):
            def unit(v, src, dv=0, n=S, first=None, rows=None):
                kc = chunks_of(v)
                hi, lo = src
                pe.wait_ge(w_split, v + 1 + 4 * dv)
                if v >= 2 or not isinstance(dv, int):
                    pe.wait_ge(evac[v % 2], v // 2 + 2 * dv)
                wh, wl = whi[v % 2], wlo[v % 2]
                outs = ((bank[v % 2], 0),) if rows is None else rows
                for dst, off in outs:
                    m = P if rows is None else 8
                    for c in range(kc):
                        if first is not None:
                            pe.wait_ge(first[0], first[1] + c + 1)
                        ws = slice(c * P + off, c * P + off + m)
                        nc.tensor.matmul(dst[0:m, 0:n], wh[:, ws], hi[:, c, :], start=c == 0, stop=False)
                        nc.tensor.matmul(dst[0:m, 0:n], wh[:, ws], lo[:, c, :], start=False, stop=False)
                        ins = nc.tensor.matmul(dst[0:m, 0:n], wl[:, ws], hi[:, c, :], start=False, stop=c == kc - 1)
                ins.then_inc(unit_done, 1)

            H, G, M = (hhi, hlo), (ghi, glo), (mem_hi, mem_lo)

            def ada(a, da=0):
                pe.wait_ge(ada_step, DC * (a + 1) + DC * da)
                col = slice(a + da, a + da + 1) if isinstance(da, int) else bass.ds(a + da, 1)
                nc.tensor.matmul(bank[7][:, col], ada_acc[a % 4], ones[:, 0:1], start=True,
                                 stop=True).then_inc(ada_done, 1)

            def norm_sum(n):
                w = width(n)
                pe.wait_ge(sq_added, (DC - 2) * (n + 1))
                nc.tensor.matmul(bank[4][:, 0:w], ones, square_sum[:, 0:w], start=True, stop=False)
                pe.wait_ge(sq_done, DC * (n + 1))
                nc.tensor.matmul(bank[4][:, 0:w], ones, square[1][:, 0:w], start=False, stop=True).then_inc(sum_done, 1)

            def swiglu(f):
                base, j0 = V_FFN[f], J_FFN[f]
                n = (N_FFN1, N_FFN2)[f]
                for part, kc in enumerate(FF_PARTS):
                    v0, j1, a0 = base + 24 * part, j0 + 8 * part, ADA_PART[part]

                    def body(i, first=None):
                        for k in range(4):
                            unit(v0 + k, H, i, first=first if k == 0 else None)
                            if f == 0 and (k >= 2 or not isinstance(i, int)):
                                ada(a0 + k - 2, 4 * i)

                    if f == 0:
                        pe.wait_ge(mods_done, (2, 6, 7)[part])
                    body(0, (h_ready, H_AT[n]) if part == 0 else None)
                    with pe.Fori(1, kc // 2) as i:
                        body(i)
                    if f == 0:
                        for a in range(a0 + 2 * kc - 2, a0 + 2 * kc):
                            ada(a)
                    for c in range(DC):
                        unit(v0 + 2 * kc + c, G, first=(op_ready, j1) if c == 0 else None)
                        if f == 0 and 2 <= c < 2 + ADA_TAIL:
                            ada(ADA_PART[part + 1] - ADA_TAIL + c - 2)

            pe.wait_ge(con_landed, 16)
            for a in range(4):
                ada(a)
            with pe.Fori(1, ADA_HEAD_N // 4) as i:
                for a in range(4):
                    ada(a, 4 * i)
            norm_sum(N_FFN1)
            swiglu(0)

            norm_sum(N_MIX)

            def rotate(j):
                v = V_MIX + j
                pe.wait_ge(evac[v % 2], v // 2 + 1)
                if j >= 2:
                    pe.wait_ge(rope_mul, 2 * (j - 1))
                nc.tensor.matmul(bank[2 + j % 2][:], rot, gate_in[j % 2][:], start=True, stop=True).then_inc(rot_done, 1)

            def turn_values(src, dst, nblk):
                for b in range(nblk):
                    ins = nc.tensor.transpose(dst[:, b * P:(b + 1) * P], src[:, b * P:(b + 1) * P], ident)
                ins.then_inc(vT_done, 1)

            for j in range(12):
                unit(V_MIX + j, H, first=(h_ready, H_AT[N_MIX]) if j == 0 else None)
                if 1 <= j <= 10:
                    rotate(j - 1)
                if j == 11:
                    v = V_MIX + 10
                    pe.wait_ge(evac[v % 2], v // 2 + 1)
                    turn_values(gate_in[0], bank[4], NB)

            def scores(i):
                g, n = divmod(i, 4)
                half, lo = (g % 2) * HD, (0 if n else P)
                if i > 0:
                    pe.wait_ge(masked, 2 * i)
                else:
                    pe.wait_ge(rope_done, 10)
                for hh in range(4):
                    ins = nc.tensor.matmul(bank[2 + hh // 2][:, (hh % 2) * 2 * P + lo:(hh % 2 + 1) * 2 * P],
                                           qT[half:half + HD, 4 * (g // 2) + hh, n * P:(n + 1) * P],
                                           kT[half:half + HD, g // 2, (n - 1) * P + lo:(n + 1) * P], start=True, stop=True)
                ins.then_inc(score_done, 1)

            def turn_probs(i, S_, kbs):
                pe.wait_ge(prob_done, i + 1)
                if i > 0:
                    pe.wait_ge(turned_out, i)
                for kb in kbs:
                    for hh in range(4):
                        ins = nc.tensor.transpose(bank[4 + kb][:, hh * P:(hh + 1) * P],
                                                  S_[i % 2][:, hh, kb * P:(kb + 1) * P], ident)
                ins.then_inc(turned, 1)

            def kbs_of(i):
                return range(0 if i % 4 else 1, 2)

            def values(i):
                g, n = divmod(i, 4)
                pe.wait_ge(turned_out, i + 1)
                if i > 0:
                    pe.wait_ge(pv_out, i)
                kbs = kbs_of(i)
                for kb in kbs:
                    ins = nc.tensor.matmul(bank[6][0:HD, :], v_tok[:, n - 1 + kb, g * HD:(g + 1) * HD], probT[:, kb, :],
                                           start=kb == kbs[0], stop=kb == 1)
                ins.then_inc(pv_done, 1)

            v = V_MIX + 11
            pe.wait_ge(evac[v % 2], v // 2 + 1)
            turn_values(gate_in[1], bank[5], NB)
            pe.wait_ge(vtok_done, 2)
            for i in range(16):
                scores(i)
                for a, v in enumerate(slot_units(i)):
                    if v < V_CP:
                        unit(v, H)
                    else:
                        unit(v, H if (v - V_CP) % 2 == 0 else G, first=(op_ready, J_Y) if v == V_CP + 1 else None)
                    if a == 0 and i > 0:
                        turn_probs(i - 1, prob, kbs_of(i - 1))
                    if a == 1 and i > 0:
                        values(i - 1)
            turn_probs(15, prob, kbs_of(15))
            values(15)
            for c in range(2 * DC):
                unit(V_AP + c, H if c % 2 == 0 else G, first=(op_ready, J_O) if c == 1 else None)
            for c in range(DC):
                unit(V_WO + c, H, first=(op_ready, J_M) if c == 0 else None)
            norm_sum(N_FFN2)
            swiglu(1)

            norm_sum(N_FINAL)
            norm_sum(N_MIX2)
            unit(V_GATE, H, first=(h_ready, H_AT[N_MIX2]), rows=((bank[V_GATE % 2], 0), (bank[2], 8)))

            def group_unit(v, last=False):
                unit(v, H)
                if v < V_ML:
                    h, k = divmod(v - V_HG, 5)
                    if k == 3:
                        pe.wait_ge(evac[v % 2], v // 2 + 1)
                        if h > 0:
                            pe.wait_ge(vtok_done, 2 + h)
                        turn_values(gate_in[0], bank[5], NB)
                else:
                    h, k = divmod(v - V_ML, 4)
                    if k == 2:
                        pe.wait_ge(evac[v % 2], v // 2 + 1)
                        turn_values(gate_in[0], bank[4], NB)

            for k in range(5):
                group_unit(V_HG + k)
                if k == 4:
                    pe.wait_ge(gate_chain, 13)
                    for dr in range(2):
                        for b in range(NB):
                            at_ = (dr * NB + b) * 8
                            ins = nc.tensor.matmul(bank[3][:, at_:at_ + 8],
                                                   row["a" if dr == 0 else "z"][0:8, b * P:(b + 1) * P],
                                                   ident[0:8, 0:8], start=True, stop=True)
                    ins.then_inc(acol_done, 1)
                    pe.wait_ge(acol_done, 2)

            def hg_items(h, zs):
                s = hg[h % 2]
                for z in zs:
                    if ITEMS * h + z >= 2:
                        pe.wait_ge(lev_taken, ITEMS * h + z - 1)
                    b = bank[2 + z % 2]
                    if z == 0:
                        pe.wait_ge(decay, EVENTS * h + 1)
                        todo = [(blk, normed[1][:, blk * P:(blk + 1) * P], s["q"][:, blk * P:(blk + 1) * P])
                                for blk in range(NB)]
                        w = P
                    elif z <= 2 * LEVELS:
                        m, dr = divmod(z - 1, 2)
                        pe.wait_ge(decay, EVENTS * h + (2 + dr if m == 0 else 4 + dr + 2 * (m - 1)))
                        qq, kk = (q_fwd, s["q"])[dr], s[f"k{dr}"]
                        todo = [(blk, kk[:, blk * P:(blk + 1) * P], qq[:, blk * P:(blk + 1) * P]) for blk in range(NB)]
                        w = P
                    elif z == 2 * LEVELS + 1:
                        pe.wait_ge(decay, EVENTS * h + 5 + 2 * (LEVELS - 1))
                        todo = [(k, s[f"k{k // 2}"][:, a * P:(a + 1) * P], (q_fwd, s["q"])[k // 2][:, t * P:(t + 1) * P])
                                for k, (a, t) in enumerate(((0, 1), (2, 3), (1, 0), (3, 2)))]
                        w = P
                    else:
                        dr = z - 2 * LEVELS - 2
                        pe.wait_ge(decay, EVENTS * h + 4 + dr + 2 * LEVELS)
                        t0 = (S // 2, 0)[dr]
                        qq = (q_fwd, s["q"])[dr][:, t0:t0 + S // 2]
                        todo = [(k, s[f"k{dr}"][:, ((0, 2)[dr] + k) * P:((0, 2)[dr] + k + 1) * P], qq) for k in range(2)]
                        w = S // 2
                    for k, lhs, rhs in todo:
                        ins = nc.tensor.matmul(b[:, k * w:(k + 1) * w], lhs, rhs, start=True, stop=True)
                    ins.then_inc(lev_done, 1)

            def head_sum(h):
                pe.wait_ge(hsq_done, h + 1)
                if NH2 - 1 <= h < 2 * NH2 - 1:
                    pe.wait_ge(vtok_done, 2 + h + 2)
                nc.tensor.matmul(bank[4][:], ones, square[0][:], start=True, stop=True).then_inc(hsum_done, 1)

            for kind, h, units in unit_groups():
                units = list(units)
                if kind == "hg":
                    s = hg[h % 2]
                    for sl in range(5):
                        if units:
                            group_unit(units.pop(0))
                        if sl == 0 and h > 0:
                            head_sum(h - 1)
                        hg_items(h, ITEM_SLOTS[sl])
                    pe.wait_ge(lev_taken, ITEMS * (h + 1))
                    if h > 0:
                        pe.wait_ge(hnorm_t, h)
                    for b in range(NB):
                        ins = nc.tensor.matmul(bank[6][:], s["v"][:, b * P:(b + 1) * P], scT[:, b * S:(b + 1) * S],
                                               start=b == 0, stop=b == NB - 1)
                    ins.then_inc(o2_done, 1)
                    if h == NH2 - 1:
                        head_sum(h)
                    continue
                s = ml[h % 2]
                for k in range(4):
                    r0 = (0, 32, 64, 96)[k]
                    if k > 0:
                        pe.wait_ge(bc_out, 4 * h + k)
                    elif h == 0:
                        pe.wait_ge(hnorm_t, NH2)
                    else:
                        pe.wait_ge(abs_done, 2 * h)
                    hd = h + 4 * (k % 2)
                    nc.tensor.matmul(bank[5][:], sel[r0:r0 + 8, hd, :], gate_rows[r0:r0 + 8, :], start=True,
                                     stop=True).then_inc(bc_done, 1)
                if h > 0:
                    head_sum(NH2 + h - 1)
                if units:
                    group_unit(units.pop(0))
                pe.wait_ge(qk_done, 2 * h + 2)
                for b in range(NB):
                    if b >= 2:
                        pe.wait_ge(s_mul, 8 * h + 2 * (b - 1))
                    elif h > 0:
                        pe.wait_ge(abs_done, 2 * h)
                    nc.tensor.matmul(bank[2 + b % 2][:], ml_k[:, b * P:(b + 1) * P], ml_q[:], start=True,
                                     stop=True).then_inc(pair_done, 1)
                    if b > 0 and units:
                        group_unit(units.pop(0))
                pe.wait_ge(s_done, 8 * h + 8)
                pe.wait_ge(bc_out, 4 * h + 4)
                if h > 0:
                    pe.wait_ge(ml_step, ML_STEPS * h)
                for dr in range(2):
                    order = range(NB) if dr == 0 else range(NB - 1, -1, -1)
                    for which in range(2):
                        dst = bank[(6, 7)[dr]] if which == 0 else bank[(5, 3)[dr]]
                        for k, b in enumerate(order):
                            t0, t1, at_ = s_range(dr, b)
                            lhs = s["v"][:, b * P:(b + 1) * P] if which == 0 else ones
                            ins = nc.tensor.matmul(dst[:, t0:t1], lhs, sT[dr][:, at_:at_ + t1 - t0], start=k == 0,
                                                   stop=k == NB - 1)
                    ins.then_inc(nd_done, 1)
                if h == NH2 - 1:
                    head_sum(NH2 + h)

            def x_turn(c):
                v = V_XV + c
                pe.wait_ge(evac[v % 2], v // 2 + 1)
                if c >= 2:
                    pe.wait_ge(vtok_done, 10 + c - 1)
                turn_values(x_vT[c % 2], bank[6 + c % 2], 2)

            for c in range(DC):
                unit(V_WO2 + c, G, first=(op_ready, J_Y2) if c == 0 else None)
            norm_sum(N_MEM)
            for c in range(2 * DC):
                unit(V_XK + c, M, n=MEM, first=(h_ready, H_AT[N_MEM]) if c == 0 else None)
                if c > DC:
                    x_turn(c - DC - 1)
            x_turn(DC - 1)
            norm_sum(N_XATTN)
            for c in range(DC + 4):
                if c < DC:
                    unit(V_XQ + c, H, first=(h_ready, H_AT[N_XATTN]) if c == 0 else None)
                if c >= 2 and c % 2 == 0 and c < DC + 2:
                    hh = c // 2 - 1
                    v = V_XQ + c - 1
                    pe.wait_ge(evac[v % 2], v // 2 + 1)
                    pe.wait_ge(evac[(v - 1) % 2], (v - 1) // 2 + 1)
                    pe.wait_ge(masked, 2 * (16 + hh))
                    for n in range(NB):
                        for e in range(2):
                            ins = nc.tensor.matmul(bank[2 + n // 2][:, (n % 2) * 2 * P:(n % 2 + 1) * 2 * P],
                                                   xq[:, 2 * hh + e, n * P:(n + 1) * P], xk[:, 2 * hh + e, :],
                                                   start=e == 0, stop=e == 1)
                    ins.then_inc(score_done, 1)
                if c >= 3 and c % 2 == 1 and c < DC + 3:
                    turn_probs(16 + (c - 3) // 2, x_prob, range(2))
                if c >= 4 and c % 2 == 0:
                    hh = c // 2 - 2
                    pe.wait_ge(turned_out, 16 + hh + 1)
                    pe.wait_ge(pv_out, 16 + hh)
                    for e in range(2):
                        for kb in range(2):
                            ins = nc.tensor.matmul(bank[6 + e][:], xv[:, kb, (2 * hh + e) * P:(2 * hh + e + 1) * P],
                                                   x_probT[:, kb, :], start=kb == 0, stop=kb == 1)
                    ins.then_inc(pv_done, 1)
            for c in range(DC):
                unit(V_XO + c, G, first=(op_ready, J_XO) if c == 0 else None)
            norm_sum(N_MLP)

            def mlp(i, first):
                for c in range(DC):
                    unit(V_MLP + c, H, 4 * i, first=first if c == 0 else None)
                for c in range(DC):
                    unit(V_MLP + DC + c, G, 4 * i, first=(op_ready, J_MLP + DC * i) if c == 0 else None)

            mlp(0, (h_ready, H_AT[N_MLP]))
            with pe.Fori(1, MLP_PARTS) as i:
                mlp(i, None)
            norm_sum(N_OUT)


def constants():
    con = np.zeros((P, N_CON), np.float32)
    i = np.arange(P)
    con[i, CON["ident"] + i] = 1
    con[:, CON["ones"]:CON["ones"] + P] = 1
    for half in (0, HD):
        k = half + np.arange(HD // 2)
        con[k + HD // 2, CON["rot"] + k] = -1
        con[k, CON["rot"] + k + HD // 2] = 1
    con[:, CON["tri"]:CON["tri"] + P] = i[:, None] <= i[None, :]
    con[:, CON["tri"] + P:CON["tri"] + 2 * P] = i[:, None] >= i[None, :]
    diff = P + i[:, None] - np.arange(2 * P)[None, :]
    con[:, CON["win"]:CON["win"] + 2 * P] = np.where((diff >= 0) & (diff < P), 0, -1e30)
    for base in (0, 32, 64, 96):
        for r in range(8):
            con[base + r, CON["sel"] + r * P:CON["sel"] + (r + 1) * P] = 1
    mask = np.zeros((P, 2 * LEVELS, P), np.float32)
    for m in range(LEVELS):
        same = (i[:, None] >> (m + 1)) == (i[None, :] >> (m + 1))
        late = (i >> m) & 1
        mask[:, 2 * m] = same & (late[:, None] == 0) & (late[None, :] == 1)
        mask[:, 2 * m + 1] = same & (late[:, None] == 1) & (late[None, :] == 0)
    inv = 1.0 / (np.float32(10000.0) ** (np.arange(0, HD, 2, dtype=np.float32) / HD))
    ang = (np.arange(S, dtype=np.float32)[:, None] * inv.astype(np.float32)[None, :]).T
    rope = np.stack([np.tile(np.cos(ang), (4, 1)), np.tile(np.sin(ang), (4, 1))], axis=1)
    return con, np.ascontiguousarray(rope, dtype=np.float32), mask


def tiles(w):
    k, n = w.shape
    return w.reshape(k // P, P, n // P, P).transpose(2, 1, 0, 3).reshape(n // P, P, k)


def feature_major(x):
    t, d = x.shape
    return np.ascontiguousarray(x.reshape(t, d // P, P).transpose(2, 1, 0))


def in_turn(*units):
    return np.stack(units, axis=1).reshape(-1, *units[0].shape[1:])


def pack(a):
    heads = np.array([[4 * (2 * m + half) + j for half in range(2)] for m in range(2) for j in range(4)]).ravel()
    order = (heads[:, None] * HD + np.arange(HD)).ravel()

    def swiglu(w_gu, w_down):
        gu = in_turn(tiles(w_gu[:, :FF]), tiles(w_gu[:, FF:]))
        out, at = [], 0
        for kc in FF_PARTS:
            out.append((gu[2 * at:2 * (at + kc)], tiles(w_down[at * P:(at + kc) * P])))
            at += kc
        return out

    ada = tiles(a["w_ada"][0])
    w8, w6 = [ada[:ADA_HEAD_N]], []
    for part, (gu, down) in enumerate(swiglu(a["w1_gu"][0], a["w1_down"][0])):
        own = ada[ADA_PART[part]:ADA_PART[part + 1]]
        w8.append(in_turn(gu, own[:len(gu)]))
        tail = own[len(gu):]
        if part < 2:
            w8 += [in_turn(down[:ADA_TAIL], tail), down[ADA_TAIL:]]
        else:
            w8.append(tail)
            w6.append(down)
    w_in = a["w_in"][0]
    b, c, u, q, k, v, zc, za = np.split(w_in, np.cumsum([D, D, D, D, 256, 256, D]), axis=1)
    w8 += [tiles(q[:, order]), tiles(k), tiles(v), in_turn(tiles(c), tiles(u), tiles(b)),
           in_turn(tiles(zc), tiles(a["w_conv_proj"][0])), in_turn(tiles(za), tiles(a["w_attn_proj"][0][order])),
           tiles(a["w_out"][0])]
    for gu, down in swiglu(a["w2_gu"][0], a["w2_down"][0]):
        w8.append(gu)
        (w8 if down.shape[2] == D else w6).append(down)
    w_in = a["w_in_2"][0]
    gates = np.zeros((D, P), np.float32)
    gates[:, :16] = w_in[:, 36 * P:]
    t = tiles(w_in[:, :36 * P]).reshape(9, 4, P, D)
    w8 += [tiles(gates), t[:5].transpose(1, 0, 2, 3).reshape(-1, P, D), t[5:].transpose(1, 0, 2, 3).reshape(-1, P, D),
           tiles(a["w_out_2"][0]), tiles(a["w_xkv_2"][0]), tiles(a["w_xq_2"][0]), tiles(a["w_xo_2"][0])]
    up = tiles(a["w_up_2"][0])
    for part in range(MLP_PARTS):
        w8 += [up[part * DC:(part + 1) * DC], tiles(a["w_down_2"][0][part * D:(part + 1) * D])]
    return np.concatenate(w8), np.concatenate(w6)


def pack_vectors(a):
    def cols(x):
        return x.reshape(-1, P).T

    vec = np.zeros((P, N_VEC), np.float32)
    gains = [a[n].reshape(-1) for n in ("g_ffn1", "g_mix", "g_ffn2", "g_final", "norm_mix_2", "norm_mem_2",
                                        "norm_xattn_2", "norm_mlp_2", "norm_final_2")]
    b_in = a["b_in_2"][0]
    for name, x in (("c", cols(a["c"])), ("b_ada", cols(a["b_ada"])), ("gain", cols(np.concatenate(gains))),
                    ("conv_w", cols(a["conv_w"])), ("b_in", cols(b_in[:36 * P])),
                    ("b_gate", b_in[36 * P:].reshape(2, 8).T), ("lb", cols(a["hgrn_lb_logits_2"])),
                    ("hgrn_g", cols(a["hgrn_norm_2"])), ("mconv_w", cols(a["mlstm_conv_w_2"])),
                    ("mconv_b", cols(a["mlstm_conv_b_2"])), ("mlstm_g", cols(a["mlstm_norm_2"])),
                    ("sinks", np.broadcast_to(a["sinks"].reshape(1, N_Q), (P, N_Q)))):
        vec[:x.shape[0], VEC[name]:VEC[name] + x.shape[1]] = x
    return vec


def kernel(**inputs):
    import concourse.bacc as bacc
    from concourse.bass_utils import run_bass_kernel_spmd

    a = {k: np.asarray(v) for k, v in inputs.items()}
    con, rope, mask = constants()
    w8, w6 = pack(a)
    arrays = {"x_t": feature_major(a["x"][0]), "mem_t": feature_major(a["mem_2"][0]), "vectors": pack_vectors(a),
              "constants": con, "rope": rope, "level_mask_in": mask, "w8": w8, "w6": w6}
    nc = bacc.Bacc("TRN2", target_bir_lowering=False, num_devices=1)
    args = [nc.dram_tensor(n, x.shape, mybir.dt.from_np(x.dtype), kind="ExternalInput").ap() for n, x in arrays.items()]
    args.append(nc.dram_tensor("y_t", (P, DC, S), F32, kind="ExternalOutput").ap())
    build(nc, *args)
    y = run_bass_kernel_spmd(nc, [arrays], core_ids=[0]).results[0]["y_t"]
    return np.ascontiguousarray(y.transpose(2, 1, 0)).reshape(1, S, D)
```
